# Optimizing a Trainium2 kernel written in Bass

```python
import jax, jax.numpy as jnp
from jax import lax
import numpy as np

D_MODEL = 1024
BATCH = 1
SEQ = 512
DEPTH = 2

N_META = 16
D_MIX = D_MODEL
LRU_WIDTH = D_MIX // 2
LRU_HEADS = 8
LRU_HEAD_DIM = LRU_WIDTH // LRU_HEADS
CONV_WIDTH = 4
LRU_C = 8.0
MLA_HEADS = 8
QK_NOPE = 64
QK_ROPE = 32
V_DIM = (D_MIX - LRU_WIDTH) // MLA_HEADS
Q_LORA = 3 * D_MODEL // 8
KV_LORA = D_MODEL // 4
IN_COLS = 2 * LRU_WIDTH + Q_LORA + KV_LORA + QK_ROPE
D_FF = 11 * D_MODEL // 4
ROPE_THETA = 10000.0
Q_BLOCK = 128
EPS = 1e-6

kernel_name = 'hymba_rglru_mla_macaron_sandwich'

def rms_norm(x, g):
    xf = x.astype(jnp.float32)
    y = xf * lax.rsqrt(jnp.mean(xf * xf, axis=-1, keepdims=True) + EPS)
    return (y * g.astype(jnp.float32)).astype(x.dtype)

def swiglu(u, w_gate, w_up, w_down):
    return (jax.nn.silu(u @ w_gate) * (u @ w_up)) @ w_down

def rope_tables(T):
    pos = jnp.arange(T, dtype=jnp.float32)
    inv_freq = 1.0 / (ROPE_THETA ** (jnp.arange(0, QK_ROPE, 2, dtype=jnp.float32) / QK_ROPE))
    ang = pos[:, None] * inv_freq[None, :]
    return jnp.cos(ang), jnp.sin(ang)

def apply_rope(x, cos, sin):
    x1, x2 = jnp.split(x, 2, axis=-1)
    cos = cos.astype(x.dtype)
    sin = sin.astype(x.dtype)
    return jnp.concatenate([x1 * cos - x2 * sin, x2 * cos + x1 * sin], axis=-1)

def _lru_combine(left, right):
    a_l, b_l = left
    a_r, b_r = right
    return a_l * a_r, a_r * b_l + b_r

def rglru_group(xr, gr, conv_w, conv_b, w_a, b_a, w_x, b_x, lam):
    B, T, W = xr.shape
    xp = jnp.pad(xr, ((0, 0), (CONV_WIDTH - 1, 0), (0, 0)))
    xc = xp[:, CONV_WIDTH - 1:] * conv_w[CONV_WIDTH - 1] + conv_b
    for k in range(CONV_WIDTH - 1):
        xc = xc + xp[:, k:k + T] * conv_w[k]
    xh = xc.reshape(B, T, LRU_HEADS, LRU_HEAD_DIM)
    r = jax.nn.sigmoid(jnp.einsum('bthi,hij->bthj', xh, w_a).reshape(B, T, W) + b_a)
    i = jax.nn.sigmoid(jnp.einsum('bthi,hij->bthj', xh, w_x).reshape(B, T, W) + b_x)
    log_a = -LRU_C * r.astype(jnp.float32) * jax.nn.softplus(-lam.astype(jnp.float32))
    a = jnp.exp(log_a)
    b = jnp.sqrt(-jnp.expm1(2.0 * log_a)) * (i * xc).astype(jnp.float32)
    _, h = lax.associative_scan(_lru_combine, (a, b), axis=1)
    return h.astype(xr.dtype) * jax.nn.gelu(gr)

def causal_block_attention(q, k, v):
    B, T, H, Dqk = q.shape
    n_blk = -(-T // Q_BLOCK)
    pad = n_blk * Q_BLOCK - T
    qb = jnp.pad(q, ((0, 0), (0, pad), (0, 0), (0, 0)))
    qb = qb.reshape(B, n_blk, Q_BLOCK, H, Dqk).transpose(1, 0, 2, 3, 4)
    scale = Dqk ** -0.5
    kpos = jnp.arange(T)

    def one_block(args):
        q_blk, blk = args
        s = jnp.einsum('bqhd,bkhd->bhqk', q_blk, k).astype(jnp.float32) * scale
        qpos = blk * Q_BLOCK + jnp.arange(Q_BLOCK)
        s = jnp.where(kpos[None, :] <= qpos[:, None], s, -jnp.inf)
        p = jax.nn.softmax(s, axis=-1).astype(v.dtype)
        return jnp.einsum('bhqk,bkhd->bqhd', p, v)

    o = lax.map(one_block, (qb, jnp.arange(n_blk)))
    o = o.transpose(1, 0, 2, 3, 4).reshape(B, n_blk * Q_BLOCK, H, v.shape[-1])
    return o[:, :T]

def mla_group(cq, ckv, kr, cos, sin, q_norm_g, w_uq, kv_norm_g, w_ukv):
    B, T, _ = cq.shape
    q = (rms_norm(cq, q_norm_g) @ w_uq).reshape(B, T, MLA_HEADS, QK_NOPE + QK_ROPE)
    q_nope, q_rope = jnp.split(q, [QK_NOPE], axis=-1)
    q_rope = apply_rope(q_rope, cos[None, :, None, :], sin[None, :, None, :])
    kv = (rms_norm(ckv, kv_norm_g) @ w_ukv).reshape(B, T, MLA_HEADS, QK_NOPE + V_DIM)
    k_nope, v = jnp.split(kv, [QK_NOPE], axis=-1)
    k_rope = apply_rope(kr, cos[None], sin[None])
    k_rope = jnp.broadcast_to(k_rope[:, :, None, :], (B, T, MLA_HEADS, QK_ROPE))
    qf = jnp.concatenate([q_nope, q_rope], axis=-1)
    kf = jnp.concatenate([k_nope, k_rope], axis=-1)
    return causal_block_attention(qf, kf, v).reshape(B, T, MLA_HEADS * V_DIM)

def setup_inputs(seed: int = 0) -> dict:
    key = jax.random.key(seed)
    ks = jax.random.split(key, 32)

    def nrm(k, shape, scale):
        return jax.random.normal(k, shape, jnp.float32) * scale

    def gain(k, n):
        return 1.0 + 0.02 * jax.random.normal(k, (DEPTH, n), jnp.float32)

    a0 = jax.random.uniform(ks[15], (DEPTH, LRU_WIDTH), jnp.float32, 0.9, 0.999)
    lam = jnp.log(a0) - jnp.log1p(-a0)
    return {
        'x': nrm(ks[0], (BATCH, SEQ, D_MODEL), 1.0),
        'meta_tokens': nrm(ks[1], (N_META, D_MODEL), 1.0),
        'ffn1_pre_g': gain(ks[2], D_MODEL),
        'ffn1_w_gate': nrm(ks[3], (DEPTH, D_MODEL, D_FF), D_MODEL ** -0.5),
        'ffn1_w_up': nrm(ks[4], (DEPTH, D_MODEL, D_FF), D_MODEL ** -0.5),
        'ffn1_w_down': nrm(ks[5], (DEPTH, D_FF, D_MODEL), D_FF ** -0.5),
        'ffn1_post_g': gain(ks[6], D_MODEL),
        'mix_pre_g': gain(ks[7], D_MODEL),
        'w_in': nrm(ks[8], (DEPTH, D_MODEL, IN_COLS), D_MODEL ** -0.5),
        'lru_conv_w': nrm(ks[9], (DEPTH, CONV_WIDTH, LRU_WIDTH), CONV_WIDTH ** -0.5),
        'lru_conv_b': nrm(ks[10], (DEPTH, LRU_WIDTH), 0.01),
        'lru_w_a': nrm(ks[11], (DEPTH, LRU_HEADS, LRU_HEAD_DIM, LRU_HEAD_DIM), LRU_HEAD_DIM ** -0.5),
        'lru_b_a': nrm(ks[12], (DEPTH, LRU_WIDTH), 0.01),
        'lru_w_x': nrm(ks[13], (DEPTH, LRU_HEADS, LRU_HEAD_DIM, LRU_HEAD_DIM), LRU_HEAD_DIM ** -0.5),
        'lru_b_x': nrm(ks[14], (DEPTH, LRU_WIDTH), 0.01),
        'lru_lambda': lam,
        'mla_q_norm_g': gain(ks[16], Q_LORA),
        'mla_w_uq': nrm(ks[17], (DEPTH, Q_LORA, MLA_HEADS * (QK_NOPE + QK_ROPE)), Q_LORA ** -0.5),
        'mla_kv_norm_g': gain(ks[18], KV_LORA),
        'mla_w_ukv': nrm(ks[19], (DEPTH, KV_LORA, MLA_HEADS * (QK_NOPE + V_DIM)), KV_LORA ** -0.5),
        'lru_out_g': gain(ks[20], LRU_WIDTH),
        'mla_out_g': gain(ks[21], MLA_HEADS * V_DIM),
        'w_out': nrm(ks[22], (DEPTH, D_MIX, D_MODEL), D_MIX ** -0.5),
        'mix_post_g': gain(ks[23], D_MODEL),
        'ffn2_pre_g': gain(ks[24], D_MODEL),
        'ffn2_w_gate': nrm(ks[25], (DEPTH, D_MODEL, D_FF), D_MODEL ** -0.5),
        'ffn2_w_up': nrm(ks[26], (DEPTH, D_MODEL, D_FF), D_MODEL ** -0.5),
        'ffn2_w_down': nrm(ks[27], (DEPTH, D_FF, D_MODEL), D_FF ** -0.5),
        'ffn2_post_g': gain(ks[28], D_MODEL),
    }

def reference(x, meta_tokens, ffn1_pre_g, ffn1_w_gate, ffn1_w_up, ffn1_w_down, ffn1_post_g,
              mix_pre_g, w_in, lru_conv_w, lru_conv_b, lru_w_a, lru_b_a, lru_w_x, lru_b_x,
              lru_lambda, mla_q_norm_g, mla_w_uq, mla_kv_norm_g, mla_w_ukv, lru_out_g,
              mla_out_g, w_out, mix_post_g, ffn2_pre_g, ffn2_w_gate, ffn2_w_up, ffn2_w_down,
              ffn2_post_g):
    B = x.shape[0]
    meta = jnp.broadcast_to(meta_tokens.astype(x.dtype)[None], (B, N_META, D_MODEL))
    h = jnp.concatenate([meta, x], axis=1)
    T = h.shape[1]
    cos, sin = rope_tables(T)
    splits = [LRU_WIDTH, 2 * LRU_WIDTH, 2 * LRU_WIDTH + Q_LORA, 2 * LRU_WIDTH + Q_LORA + KV_LORA]
    for l in range(DEPTH):
        f = swiglu(rms_norm(h, ffn1_pre_g[l]), ffn1_w_gate[l], ffn1_w_up[l], ffn1_w_down[l])
        h = h + 0.5 * rms_norm(f, ffn1_post_g[l])
        z = rms_norm(h, mix_pre_g[l]) @ w_in[l]
        xr, gr, cq, ckv, kr = jnp.split(z, splits, axis=-1)
        y_lru = rglru_group(xr, gr, lru_conv_w[l], lru_conv_b[l], lru_w_a[l], lru_b_a[l],
                            lru_w_x[l], lru_b_x[l], lru_lambda[l])
        y_mla = mla_group(cq, ckv, kr, cos, sin, mla_q_norm_g[l], mla_w_uq[l],
                          mla_kv_norm_g[l], mla_w_ukv[l])
        y = jnp.concatenate([rms_norm(y_lru, lru_out_g[l]), rms_norm(y_mla, mla_out_g[l])],
                            axis=-1) @ w_out[l]
        h = h + rms_norm(y, mix_post_g[l])
        f = swiglu(rms_norm(h, ffn2_pre_g[l]), ffn2_w_gate[l], ffn2_w_up[l], ffn2_w_down[l])
        h = h + 0.5 * rms_norm(f, ffn2_post_g[l])
    return h[:, N_META:]


_drawn_inputs = setup_inputs


def setup_inputs(seed=0):
    import zlib

    import numpy as np

    out = dict(_drawn_inputs(seed))
    spreads = {}
    factors = {'ffn1_post_g': 3.663,
     'lru_b_a': 8.0,
     'lru_b_x': 8.0,
     'mla_q_norm_g': 5.115,
     'mla_kv_norm_g': 2.955,
     'lru_out_g': 4.353,
     'mla_out_g': 3.52,
     'mix_post_g': 2.733,
     'ffn2_pre_g': 4.573,
     'ffn2_post_g': 6.329}
    for name, (base, spread) in spreads.items():
        noise = np.random.default_rng([zlib.crc32(name.encode()), seed]).standard_normal(out[name].shape)
        drawn = base * np.exp(spread * noise) if base else spread * noise
        out[name] = __import__('jax').numpy.asarray(drawn.astype(out[name].dtype))
    for name, factor in factors.items():
        out[name] = (out[name] * factor).astype(out[name].dtype)
    return out
```

```python
from contextlib import ExitStack

import numpy as np

import concourse.bass as bass
from concourse import mybir

F32 = mybir.dt.float32
F32R = mybir.dt.float32r
BF16 = mybir.dt.bfloat16
ALU = mybir.AluOpType
ACT = mybir.ActivationFunctionType
AX = mybir.AxisListType

P = 128
EPS = 1e-6
LRU_C = 8.0
N_META = 16
SEQ = 512
T = N_META + SEQ
HALF = T // 2
D = 1024
DC = D // P
CONV = 4
W = 512
WC = W // P
HEADS = 8
NOPE = 64
ROPE = 32
VD = 64
QL = 384
QC = QL // P
KVL = 256
KVC = KVL // P
ROPE_THETA = 10000.0
RING = 4
MASKED = -1e30

PARAMS = [
    ("ffn1_pre_g", DC), ("ffn1_post_g", DC), ("mix_pre_g", DC), ("mix_post_g", DC),
    ("ffn2_pre_g", DC), ("ffn2_post_g", DC), ("lru_conv_w", CONV * WC), ("lru_conv_b", WC),
    ("lru_b_a", WC), ("lru_b_x", WC), ("lru_lambda", WC), ("mla_q_norm_g", QC),
    ("mla_kv_norm_g", KVC), ("lru_out_g", WC), ("mla_out_g", WC),
]
PCOL = {}
NPAR = 0
for _name, _n in PARAMS:
    PCOL[_name] = NPAR
    NPAR += _n

C_ID, C_ONE, C_SEL, C_MASK, C_EPS, C_LNS, NCONST = 0, P, 2 * P, 3 * P, 4 * P, 4 * P + 1, 4 * P + 2

S_XR, S_CQ, S_GATE, S_CKV, S_KR, S_GR, S_V, S_K, S_Q, S_OUT = 0, 4, 7, 8, 10, 11, 15, 16, 17, 21
MIX_TILES = [DC] * 7 + [2 * WC] + [DC] * 7 + [KVC * 4] + [4 * KVC] + [2 * QC] * 4 + [DC] * DC


def build_program(nc, a, out, depth, d_ff):
    FC = d_ff // P
    FH = FC // 2
    MAXT = max(FH, DC)
    NB = 3 * depth
    assert FC % 2 == 0 and FC >= 6

    ffn_slots = 2 * FC + 2 * DC
    tiles = []
    slot0 = []
    for b in range(NB):
        slot0.append(len(tiles))
        tiles += MIX_TILES if b % 3 == 1 else [DC] * (2 * FC) + [FH] * (2 * DC)
    NSLOT = len(tiles)
    MIX_UNITS = dict(xr=WC, cq=QC, gate=2 * WC, ckv=KVC, statq=1, kr=1, statkv=1, gr=WC, sel=1,
                     v=3, k=4, qa=2, statl=1, qb=HEADS - 2, tr=WC, out=DC)
    U = {}
    n = 0
    for b in range(NB):
        if b:
            U[b, "post"] = n
            n += 1
        U[b, "pre"] = n
        n += 1
        parts = MIX_UNITS if b % 3 == 1 else dict(gu=2 * FC, out=DC)
        for name, k in parts.items():
            U[b, name] = n
            n += k
    U[NB, "post"] = n

    def trimmed(b):
        return b >= NB - 2

    def unit_q(b, hd):
        return U[b, "qa"] + hd if hd < 2 else U[b, "qb"] + hd - 2

    def pair_of(u):
        return u % 4

    def free_for(u):
        return u // 4 + 1

    def read_out(u):
        return u // 4 + 2

    def slot_used(n):
        return n + 1 + RING

    with ExitStack() as ctx:
        def sem(name):
            return ctx.enter_context(nc.semaphore(name))

        base = [(nc.sbuf_base + 31) // 32 * 32]

        def sb_at(name, offset, shape, dt):
            return nc.alloc_sbuf_tensor_at(name, shape, dt, offset=offset)

        def sb(name, shape, dt):
            size = 2 if dt == BF16 else 4
            for s in shape[1:]:
                size *= s
            t = sb_at(name, base[0], shape, dt)
            base[0] += (size + 31) // 32 * 32
            return t

        CH = T * 4
        h = sb("h", [P, DC, T], F32)
        xh_at = base[0]
        xh = sb("xh", [P, DC, T], F32R)
        xl_at = base[0]
        xl = sb("xl", [P, DC, T], F32R)
        f_ffn = sb_at("f_ffn", xl_at, [P, DC, T], F32)
        raw = sb("raw", [P, RING, MAXT * P], F32)
        whi = sb("whi", [P, RING, MAXT * P], F32R)
        wlo = sb("wlo", [P, RING, MAXT * P], F32R)
        par = sb("par", [P, depth, NPAR], F32)
        half_g = sb("half_g", [P, depth, 2, DC], F32)
        half_b = sb("half_b", [P, depth, 2, WC], F32)
        decay = sb("decay", [P, 2, depth, WC], F32)
        consts = sb("consts", [P, NCONST], F32)
        identb = sb("identb", [P, P], BF16)
        maskb = sb("maskb", [P, P], BF16)
        rs_in = sb("rs_in", [P, T], F32)
        tmp = [sb(f"tmp{i}", [P, T], F32) for i in range(5)]
        small = sb("small", [P, 64], F32)
        arena = base[0]

        hidh = sb_at("hidh", arena, [P, FC, T], F32R)
        hidl = sb_at("hidl", arena + FC * CH, [P, FC, T], F32R)
        off = [arena]

        def over(name, shape, dt, at=None):
            t = sb_at(name, off[0] if at is None else at, shape, dt)
            if at is None:
                size = 4
                for s in shape[1:]:
                    size *= s
                off[0] += (size + 31) // 32 * 32
            return t

        xr_at = off[0]
        xr = over("xr", [P, WC, T + CONV - 1], F32)
        rg = over("rg", [P, WC, T], F32, xr_at)
        ylh = over("ylh", [P, WC, T], F32R, xr_at)
        gr_at = off[0]
        gr = over("gr", [P, WC, T], F32)
        xc = over("xc", [P, WC, T], F32)
        xch_at = off[0]
        xch = over("xch", [P, WC, T], F32R)
        xcl = over("xcl", [P, WC, T], F32R)
        vt = over("vt", [P, 5, HEADS * VD], F32, xch_at)
        ig_at = off[0]
        ig = over("ig", [P, WC, T], F32)
        av_at = off[0]
        av = over("av", [P, WC, T], F32)
        yll = over("yll", [P, WC, T], F32R, av_at)
        cq_at = off[0]
        cqh = over("cqh", [P, QC, T], F32R)
        cql = over("cql", [P, QC, T], F32R)
        osb = over("osb", [P, 4, HEADS * VD], F32, cq_at)
        osb0 = over("osb0", [P, HEADS * VD], F32, cq_at + 4 * HEADS * VD * 4)
        z_at = off[0]
        cq = over("cq", [P, QC, T], F32)
        ckv = over("ckv", [P, KVC, T], F32)
        ckvh = over("ckvh", [P, KVC, T], F32R)
        ckvl = over("ckvl", [P, KVC, T], F32R)
        assert 4 * HEADS * VD * 4 + HEADS * VD * 4 <= 2 * QC * CH
        prob = [over(f"prob{i}", [P, T], F32, z_at + c * CH) for i, c in enumerate((0, 1, 3))]
        probT = [over(f"probT{i}", [P, 5 * P], F32, z_at + 4 * CH + i * 5 * P * 4) for i in range(3)]
        assert 4 * CH + 3 * 5 * P * 4 <= (QC + 3 * KVC) * CH
        ropet = [over("ropet0", [P, T], F32, z_at + 2 * CH), over("ropet1", [P, T], F32)]
        kt_of = [sb_at(f"kt{i}", at, [P, 4, T], F32) for i, at in enumerate((xh_at, xl_at))]
        qt_of = [sb_at(f"qt{i}", at + 4 * CH, [P, 4, T], F32) for i, at in enumerate((xh_at, xl_at))]
        f_mix = [sb_at(f"f_mix{i}", at, [P, WC, T], F32) for i, at in enumerate((gr_at, ig_at))]
        end = max(off[0], arena + 2 * FC * CH)
        assert end <= nc.sbuf_usable_end, end

        def kt(hd):
            return kt_of[hd % 2][:, hd // 2, :]

        def qt(hd):
            return qt_of[hd % 2][:, hd // 2, :]

        def f(b, k):
            return f_mix[k // WC][:, k % WC, :] if b % 3 == 1 else f_ffn[:, k, :]

        ps = ctx.enter_context(nc.psum_tensor("ps", [P, 8 * 512], F32))

        def pair(i):
            return ps[:, i * 1024:(i + 1) * 1024]

        ident = consts[:, C_ID:C_ID + P]
        ones = consts[:, C_ONE:C_ONE + P]
        sel = consts[:, C_SEL:C_SEL + P]
        eps = consts[:, C_EPS:C_EPS + 1]
        ln_scale = consts[:, C_LNS:C_LNS + 1]

        def col(name, l, k, p=P):
            c = PCOL[name] + k
            return par[0:p, l, c:c + 1]

        def toks(t2, trim):
            return t2[:, N_META:T] if trim else t2[:, 0:T]

        def halves(t2, trim):
            return t2[:, N_META:T] if trim else t2[:, 0:T].rearrange("p (a b) -> p a b", a=2)

        def unit(u, trim):
            if trim:
                return pair(pair_of(u))[:, 0:SEQ]
            return pair(pair_of(u)).rearrange("p (a b) -> p a b", a=2)[:, :, 0:HALF]

        def groups(trim):
            return [(N_META, SEQ, 0)] if trim else [(0, HALF, 0), (HALF, HALF, 512)]

        consts_in = sem("consts_in")
        h_in = sem("h_in")
        rope0_in = sem("rope0_in")
        rope1_in = sem("rope1_in")
        raw_full = [sem(f"raw_full{i}") for i in range(RING)]
        hi_ready = sem("hi_ready")
        lo_ready = sem("lo_ready")
        slots_used = sem("slots_used")
        psum_free = [sem(f"psum_free{i}") for i in range(4)]
        act_chain = sem("act_chain")
        dve_chain = sem("dve_chain")
        pool_chain = sem("pool_chain")
        setup_done = sem("setup_done")
        setup_exp = sem("setup_exp")
        sp_ready = sem("sp_ready")
        sq_ready = sem("sq_ready")
        sum_ready = sem("sum_ready")
        stat_post = sem("stat_post")
        rs_post = sem("rs_post")
        h_ready = sem("h_ready")
        xh_ready = sem("xh_ready")
        xl_ready = sem("xl_ready")
        hsq_ready = sem("hsq_ready")
        hsum_ready = sem("hsum_ready")
        stat_pre = sem("stat_pre")
        rs_pre = sem("rs_pre")
        silu_ready = sem("silu_ready")
        hid_ready = sem("hid_ready")
        hidh_ready = sem("hidh_ready")
        hidl_ready = sem("hidl_ready")
        xc_ready = sem("xc_ready")
        xch_ready = sem("xch_ready")
        xcl_ready = sem("xcl_ready")
        qsum_ready = sem("qsum_ready")
        kvsum_ready = sem("kvsum_ready")
        cqh_ready = sem("cqh_ready")
        cql_ready = sem("cql_ready")
        stat_mix = sem("stat_mix")
        rs_q = sem("rs_q")
        rs_kv = sem("rs_kv")
        ckvn_ready = sem("ckvn_ready")
        ckvh_ready = sem("ckvh_ready")
        ckvl_ready = sem("ckvl_ready")
        gate_mm = sem("gate_mm")
        decay_ready = sem("decay_ready")
        lru_c = sem("lru_c")
        lru_root = sem("lru_root")
        gelu_ready = sem("gelu_ready")
        y_ready = sem("y_ready")
        ysq_ready = sem("ysq_ready")
        lsum_ready = sem("lsum_ready")
        rs_lru = sem("rs_lru")
        yn_ready = sem("yn_ready")
        ylh_ready = sem("ylh_ready")
        yll_ready = sem("yll_ready")
        kr_ready = sem("kr_ready")
        sel_mm = sem("sel_mm")
        kr4_ready = sem("kr4_ready")
        krope_ready = sem("krope_ready")
        v_mm = sem("v_mm")
        k_mm = sem("k_mm")
        q_mm = sem("q_mm")
        s0_mm = sem("s0_mm")
        s0_max = sem("s0_max")
        s0_exp = sem("s0_exp")
        t0_mm = sem("t0_mm")
        t0_copied = sem("t0_copied")
        o0_mm = sem("o0_mm")
        s_mm = sem("s_mm")
        max_ready = sem("max_ready")
        prob_ready = sem("prob_ready")
        t_mm = sem("t_mm")
        t_act = sem("t_act")
        t_dve = sem("t_dve")
        pv_mm = sem("pv_mm")
        o_copied = sem("o_copied")
        osq_ready = sem("osq_ready")
        rs_att = sem("rs_att")
        on_ready = sem("on_ready")
        tr_mm = sem("tr_mm")
        yah_ready = sem("yah_ready")
        yal_ready = sem("yal_ready")
        out_done = sem("out_done")

        class Chain:

            def __init__(self, eng, s):
                self.eng, self.s, self.n = eng, s, 0

            def link(self, ins):
                self.n += 1
                ins.then_inc(self.s, 1)
                self.eng.wait_ge(self.s, self.n)

        NSUM = DC - 2
        NHSUM = DC - 1
        NQ = 4
        ITEMS = HEADS * NQ

        def keys_of(i):
            return N_META + i * P

        def copied_by_act(i):
            return i <= 2

        def block_of(j):
            return (0, N_META) if j == 0 else (N_META + (j - 1) * P, P)

        def n_meta_layers(l):
            return l

        block = ctx.enter_context(nc.Block())

        @block.sync
        def _(sp):
            def load(n, src, adv=0):
                sp.wait_ge(slots_used, n + 1 + adv)
                k = tiles[n] * P
                sp.dma_start(raw[:, n % RING, 0:k], src).then_inc(raw_full[n % RING], 16)

            for b in range(NB):
                l, s0 = b // 3, slot0[b]
                if b % 3 == 1:
                    for n in range(S_OUT):
                        if n < S_GATE:
                            src = a["w_in"][l, n]
                        elif n == S_GATE:
                            src = a["w_gates"][l]
                        elif n < S_V:
                            src = a["w_in"][l, n - 1]
                        elif n == S_V:
                            src = a["w_v"][l]
                        elif n == S_K:
                            src = a["w_k"][l]
                        else:
                            src = a["w_q"][l, n - S_Q]
                        load(s0 + n, src)
                        if n == RING:
                            sp.dma_start(ropet[1][:, :], a["rope"][1]).then_inc(rope1_in, 16)
                        if n == S_V:
                            sp.wait_ge(cql_ready, QC * (l + 1))
                            sp.dma_start(ropet[0][:, :], a["rope"][0]).then_inc(rope0_in, 16)
                    with sp.Fori(0, DC // 4) as j:
                        for m in range(4):
                            load(s0 + S_OUT + m, a["w_out"][l, j * 4 + m], j * 4)
                else:
                    name = "ffn1" if b % 3 == 0 else "ffn2"
                    with sp.Fori(0, FC // 2) as j:
                        for m in range(2):
                            load(s0 + 2 * m, a[name + "_gate"][l, j * 2 + m], j * 4)
                            load(s0 + 2 * m + 1, a[name + "_up"][l, j * 2 + m], j * 4)
                    with sp.Fori(0, DC // 2) as j:
                        for m in range(2):
                            for q in range(2):
                                load(s0 + 2 * FC + 2 * m + q, a[name + "_down"][l, j * 2 + m, q], j * 4)
            for k in range(DC):
                sp.wait_ge(h_ready, DC * (NB - 1) + k + 1)
                sp.dma_start(out[k], h[:, k, N_META:T]).then_inc(out_done, 16)
            sp.wait_ge(out_done, 16 * DC)

        @block.gpsimd
        def _(pool):
            def lo(n, adv=0):
                pool.wait_ge(hi_ready, n + 1 + adv)
                r, k = n % RING, tiles[n] * P
                nc.gpsimd.tensor_tensor(wlo[:, r, 0:k], raw[:, r, 0:k], whi[:, r, 0:k].bitcast(F32),
                                        ALU.subtract).then_inc(lo_ready, 1)

            def lo_run(first, last):
                n = first
                while n < last:
                    k = n
                    while k < last and tiles[k] == tiles[n]:
                        k += 1
                    rounds = (k - n) // RING
                    if rounds > 1:
                        with pool.Fori(0, rounds) as j:
                            for m in range(RING):
                                lo(n + m, j * RING)
                        n += rounds * RING
                    while n < k:
                        lo(n)
                        n += 1

            def square_sum(b):
                trim = b > 0 and trimmed(b - 1)
                hs = toks(tmp[4], trim)
                for k in range(1, DC):
                    pool.wait_ge(hsq_ready, DC * b + k + 1)
                    if k > 1:
                        pool.wait_ge(hsum_ready, NHSUM * b + k - 1)
                    nc.gpsimd.tensor_tensor(hs, hs, toks(tmp[k % 2], trim), ALU.add).then_inc(hsum_ready, 1)

            lo_run(0, RING)
            for b in range(NB):
                square_sum(b)
                lo_run(slot0[b] + RING, min(NSLOT, (slot0[b + 1] if b + 1 < NB else NSLOT) + RING))

        @block.scalar
        def _(act):
            chain = Chain(act, act_chain)
            act.dma_start(consts[:, :], a["consts"]).then_inc(consts_in, 16)
            act.dma_start(par[:, :, :], a["params"]).then_inc(consts_in, 16)
            for k in range(DC):
                act.dma_start(h[:, k, :], a["x"][k]).then_inc(h_in, 16)

            def hi(n, adv=0):
                if n < NSLOT:
                    r, k = n % RING, tiles[n] * P
                    act.wait_ge(raw_full[r], 16 * (n // RING + 1) + adv * 4)
                    nc.scalar.activation(whi[:, r, 0:k], raw[:, r, 0:k], ACT.Copy).then_inc(hi_ready, 1)

            def inv_rms(dst, u, n, trim=False, bias=0.0):
                nc.scalar.activation(halves(dst, trim), unit(u, trim), ACT.Ln, scale=1.0 / n,
                                     bias=eps).then_inc(psum_free[pair_of(u)], 1)
                act.wait_ge(psum_free[pair_of(u)], read_out(u))
                return nc.scalar.activation(toks(dst, trim), toks(dst, trim), ACT.Exp, scale=-0.5, bias=bias)

            def split_in(b):
                l, trim = b // 3, b > 0 and trimmed(b - 1)
                g = ("ffn1_pre_g", "mix_pre_g", "ffn2_pre_g")[b % 3]
                for k in range(DC):
                    if b == 0:
                        if k == 0:
                            act.wait_ge(h_in, 16 * DC)
                    else:
                        act.wait_ge(h_ready, DC * (b - 1) + k + 1)
                    nc.scalar.activation(toks(xh[:, k, :], trim), toks(h[:, k, :], trim), ACT.Copy,
                                         scale=col(g, l, k)).then_inc(xh_ready, 1)
                    if k >= 3:
                        act.wait_ge(hsum_ready, NHSUM * b + k - 2)
                    nc.scalar.activation(toks(tmp[k % 2 if k else 4], trim), toks(h[:, k, :], trim),
                                         ACT.Square).then_inc(hsq_ready, 1)

            def rs_pre_of(b):
                act.wait_ge(stat_pre, b + 1)
                inv_rms(rs_in, U[b, "pre"], D, b > 0 and trimmed(b - 1)).then_inc(rs_pre, 1)

            def output_chunk(b, m, last_slot):
                l, trim, u = b // 3, trimmed(b), U[b, "out"] + m
                act.wait_ge(slots_used, slot_used(last_slot))
                if m >= 3:
                    act.wait_ge(sum_ready, NSUM * b + m - 2)
                sq = tmp[4] if m == 0 else tmp[m % 2]
                nc.scalar.activation(halves(sq, trim), unit(u, trim), ACT.Square).then_inc(sq_ready, 1)
                if b % 3 == 1:
                    g = col("mix_post_g", l, m)
                else:
                    g = half_g[:, l, b % 3 // 2, m:m + 1]
                nc.scalar.activation(halves(f(b, m), trim), unit(u, trim), ACT.Copy,
                                     scale=g).then_inc(psum_free[pair_of(u)], 1)

            def rs_post_of(b):
                act.wait_ge(stat_post, b + 1)
                inv_rms(tmp[2], U[b + 1, "post"], D, trimmed(b)).then_inc(rs_post, 1)

            for n in range(RING):
                hi(n)
            act.wait_ge(setup_done, 1)
            nc.scalar.activation(small[:, 0:depth * WC], small[:, 0:depth * WC], ACT.Exp,
                                 scale=-1.0).then_inc(setup_exp, 1)

            def ffn(b):
                s0, f0 = slot0[b], (b // 3 * 2 + b % 3 // 2) * FC
                u0, trim = U[b, "gu"], b > 0 and trimmed(b - 1)

                def hidden(m, it=0):
                    adv = it * RING
                    ug = u0 + 2 * m
                    mm = m + 2 * it
                    act.wait_ge(psum_free[pair_of(ug)], read_out(ug) + it)
                    nc.scalar.activation(toks(tmp[2], trim), toks(tmp[0], trim), ACT.Silu).then_inc(silu_ready, 1)
                    hi(s0 + 2 * m + RING, adv)
                    act.wait_ge(hid_ready, f0 + mm + 1)
                    nc.scalar.activation(toks(hidh[:, mm, :], trim), toks(tmp[3], trim),
                                         ACT.Copy).then_inc(hidh_ready, 1)
                    hi(s0 + 2 * m + 1 + RING, adv)

                hidden(0)
                hidden(1)
                with act.Fori(0, FC // 2 - 2) as j:
                    hidden(2, j)
                    hidden(3, j)
                hidden(FC - 2)
                hidden(FC - 1)
                for m in range(DC):
                    q = s0 + 2 * FC + 2 * m
                    hi(q + RING)
                    output_chunk(b, m, q + 1)
                    hi(q + 1 + RING)

            def mixer(b):
                l, s0 = b // 3, slot0[b]
                hi(s0 + 4)
                hi(s0 + 5)
                for c in range(WC):
                    act.wait_ge(xc_ready, WC * l + c + 1)
                    nc.scalar.activation(xch[:, c, :], xc[:, c, :], ACT.Copy).then_inc(xch_ready, 1)
                    if c < 3:
                        hi(s0 + 6 + c)
                hi(s0 + 9)
                hi(s0 + 10)
                for c in range(QC):
                    u = U[b, "cq"] + c
                    act.wait_ge(psum_free[pair_of(u)], read_out(u))
                    nc.scalar.activation(cqh[:, c, :], cq[:, c, :], ACT.Copy,
                                         scale=col("mla_q_norm_g", l, c)).then_inc(cqh_ready, 1)
                for g, dst in enumerate((rg, ig)):
                    for c in range(WC):
                        u = U[b, "gate"] + WC * g + c
                        if WC * g + c < 2 * WC - 1:
                            act.wait_ge(gate_mm, (2 * WC - 1) * l + WC * g + c + 1)
                        else:
                            act.wait_ge(slots_used, slot_used(s0 + S_GATE))
                        nc.scalar.activation(halves(dst[:, c, :], False), unit(u, False), ACT.Tanh,
                                             scale=0.5, bias=half_b[:, l, g, c:c + 1])\
                            .then_inc(psum_free[pair_of(u)], 1)
                hi(s0 + 11)
                for c in range(WC):
                    u = U[b, "gate"] + c
                    A, nA = decay[:, 0, l, c:c + 1], decay[:, 1, l, c:c + 1]
                    act.wait_ge(psum_free[pair_of(u)], read_out(u))
                    nc.scalar.activation(av[:, c, :], rg[:, c, :], ACT.Exp, scale=A, bias=A)\
                        .then_inc(decay_ready, 1)
                    nc.scalar.activation(rg[:, c, :], rg[:, c, :], ACT.Tanh, scale=nA, bias=nA)\
                        .then_inc(decay_ready, 1)
                hi(s0 + 12)
                hi(s0 + 13)
                act.wait_ge(stat_mix, 3 * l + 1)
                inv_rms(tmp[2], U[b, "statq"], QL, bias=ln_scale).then_inc(rs_q, 1)
                hi(s0 + 14)
                act.wait_ge(stat_mix, 3 * l + 2)
                inv_rms(tmp[3], U[b, "statkv"], KVL).then_inc(rs_kv, 1)
                for c in range(KVC):
                    act.wait_ge(ckvn_ready, KVC * l + c + 1)
                    nc.scalar.activation(ckvh[:, c, :], ckv[:, c, :], ACT.Copy,
                                         scale=col("mla_kv_norm_g", l, c)).then_inc(ckvh_ready, 1)
                hi(s0 + 15)
                for c in range(WC):
                    act.wait_ge(lru_c, WC * l + c + 1)
                    nc.scalar.activation(rg[:, c, :], rg[:, c, :], ACT.Sqrt, scale=0.25)\
                        .then_inc(lru_root, 1)
                for n in (16, 17, 18):
                    hi(s0 + n)
                for c in range(WC):
                    u = U[b, "gr"] + c
                    act.wait_ge(psum_free[pair_of(u)], read_out(u))
                    nc.scalar.activation(gr[:, c, :], gr[:, c, :], ACT.Gelu_apprx_tanh)\
                        .then_inc(gelu_ready, 1)
                act.wait_ge(sel_mm, l + 1)
                u = U[b, "sel"]
                nc.scalar.activation(halves(tmp[0], False), unit(u, False), ACT.Copy)\
                    .then_inc(psum_free[pair_of(u)], 1)
                for i in range(3):
                    u = U[b, "v"] + i
                    if i < 2:
                        act.wait_ge(v_mm, 2 * l + i + 1)
                    else:
                        act.wait_ge(slots_used, slot_used(s0 + S_V))
                    n = 2 if i < 2 else 1
                    nc.scalar.activation(vt[:, 2 * i:2 * i + n, :],
                                         pair(pair_of(u)).rearrange("p (a b) -> p a b", a=2)[:, 0:n, :],
                                         ACT.Copy).then_inc(psum_free[pair_of(u)], 1)
                hi(s0 + 19)
                for i in range(HEADS // 2):
                    u = U[b, "k"] + i
                    if i < HEADS // 2 - 1:
                        act.wait_ge(k_mm, (HEADS // 2 - 1) * l + i + 1)
                    else:
                        act.wait_ge(slots_used, slot_used(s0 + S_K))
                    nc.scalar.activation(halves(kt(2 * i)[0:NOPE], False), unit(u, False)[0:NOPE],
                                         ACT.Copy)
                    nc.scalar.activation(halves(kt(2 * i + 1)[NOPE:P], False), unit(u, False)[NOPE:P],
                                         ACT.Copy).then_inc(psum_free[pair_of(u)], 1)
                hi(s0 + 20)
                for c in range(WC):
                    act.wait_ge(y_ready, WC * l + c + 1)
                    nc.scalar.activation(ig[:, c, :], xc[:, c, :], ACT.Square).then_inc(ysq_ready, 1)
                act.wait_ge(stat_mix, 3 * l + 3)
                inv_rms(tmp[4], U[b, "statl"], W).then_inc(rs_lru, 1)
                for c in range(WC):
                    act.wait_ge(yn_ready, WC * l + c + 1)
                    nc.scalar.activation(ylh[:, c, :], xc[:, c, :], ACT.Copy,
                                         scale=col("lru_out_g", l, c)).then_inc(ylh_ready, 1)
                for n in (21, 22, 23, 24):
                    hi(s0 + n)

                if not trimmed(b):
                    m0 = n_meta_layers(l)
                    act.wait_ge(s0_max, 2 * m0 + 2)
                    nc.scalar.activation(prob[0][0:N_META, 0:P], prob[0][0:N_META, 0:P], ACT.Exp)\
                        .then_inc(s0_exp, 1)
                for e in range(ITEMS + 1):
                    if e < ITEMS:
                        E, i = ITEMS * l + e, e % NQ + 1
                        nk = keys_of(i)
                        pr = pair(e % 3)
                        src = (pr[:, 0:nk] if i < NQ else
                               pr.rearrange("p (a b) -> p a b", a=2)[:, :, 0:HALF])
                        dst = (prob[e % 3][:, 0:nk] if i < NQ else halves(prob[e % 3], False))
                        act.wait_ge(max_ready, E + 1)
                        if e >= 3:
                            act.wait_ge(t_mm, E - 2)
                        nc.scalar.activation(dst, src, ACT.Exp, bias=small[:, 8 + e % 4:9 + e % 4],
                                             accum_out=small[:, 16 + e % 8:17 + e % 8])\
                            .then_inc(prob_ready, 1)
                    if e >= 1 and copied_by_act((e - 1) % NQ + 1):
                        transposed_copy_act(l, e - 1)
                act.wait_ge(o_copied, HEADS * (l + 1))
                for i in range(NQ):
                    nc.scalar.activation((prob[i] if i < 3 else probT[0])[:, 0:W], osb[:, i, :], ACT.Square,
                                         accum_out=small[:, 24 + i:25 + i]).then_inc(osq_ready, 1)
                n_sq = NQ
                if not trimmed(b):
                    nc.scalar.activation(probT[1][0:N_META, 0:W], osb0[0:N_META, :], ACT.Square,
                                         accum_out=small[0:N_META, 28:29]).then_inc(osq_ready, 1)
                    n_sq += 1
                act.wait_ge(osq_ready, NQ * l + n_meta_layers(l) + n_sq)
                chain.link(nc.scalar.activation(small[:, 32:36], small[:, 24:28], ACT.Ln,
                                                scale=1.0 / W, bias=eps))
                if not trimmed(b):
                    chain.link(nc.scalar.activation(small[0:N_META, 36:37], small[0:N_META, 28:29], ACT.Ln,
                                                    scale=1.0 / W, bias=eps[0:N_META]))
                    chain.link(nc.scalar.activation(small[0:N_META, 36:37], small[0:N_META, 36:37],
                                                    ACT.Exp, scale=-0.5))
                nc.scalar.activation(small[:, 32:36], small[:, 32:36], ACT.Exp, scale=-0.5)\
                    .then_inc(rs_att, 1)
                for c in range(WC):
                    act.wait_ge(tr_mm, WC * l + c + 1)
                    pr, g = pair(pair_of(U[b, "tr"] + c)), col("mla_out_g", l, c)
                    if not trimmed(b):
                        nc.scalar.activation(xh[:, WC + c, 0:N_META], pr[:, 512:512 + N_META], ACT.Copy,
                                             scale=g)
                    nc.scalar.activation(xh[:, WC + c, N_META:T], pr[:, 0:SEQ], ACT.Copy, scale=g)\
                        .then_inc(yah_ready, 1)
                for m in range(DC):
                    output_chunk(b, m, s0 + S_OUT + m)
                    hi(s0 + S_OUT + m + RING)

            def transposed_copy_act(l, e):
                E, i = ITEMS * l + e, e % NQ + 1
                act.wait_ge(t_mm, E + 1)
                if e >= 3:
                    act.wait_ge(pv_mm, E - 2)
                nc.scalar.activation(probT[e % 3][:, 0:(i + 1) * P], pair(e % 3)[:, 0:(i + 1) * P],
                                     ACT.Copy).then_inc(t_act, 1)

            for b in range(NB):
                split_in(b)
                rs_pre_of(b)
                if b % 3 == 1:
                    mixer(b)
                else:
                    ffn(b)
                rs_post_of(b)

        @block.vector
        def _(dve):
            chain = Chain(dve, dve_chain)
            dve.wait_ge(consts_in, 32)
            lam = par[:, :, PCOL["lru_lambda"]:PCOL["lru_lambda"] + WC]

            def sm(i):
                return small[:, i * depth * WC:(i + 1) * depth * WC].rearrange("p (l c) -> p l c", l=depth)

            chain.link(nc.vector.tensor_scalar(sm(1), lam, -1.0, None, ALU.mult))
            nc.vector.tensor_tensor(sm(0), lam, sm(1), ALU.max).then_inc(setup_done, 1)
            for i, name in enumerate(("ffn1_post_g", "ffn2_post_g")):
                nc.vector.tensor_scalar(half_g[:, :, i, :], par[:, :, PCOL[name]:PCOL[name] + DC],
                                        0.5, None, ALU.mult)
            for i, name in enumerate(("lru_b_a", "lru_b_x")):
                nc.vector.tensor_scalar(half_b[:, :, i, :], par[:, :, PCOL[name]:PCOL[name] + WC],
                                        0.5, None, ALU.mult)
            nc.vector.tensor_copy(identb[:, :], ident)
            nc.vector.tensor_copy(maskb[:, :], consts[:, C_MASK:C_MASK + P])
            chain.link(nc.vector.tensor_scalar(sm(1), sm(1), 0.0, None, ALU.max))
            dve.wait_ge(setup_exp, 1)
            chain.link(nc.vector.tensor_scalar(sm(2), sm(0), 2.0, None, ALU.add))
            chain.link(nc.vector.reciprocal(sm(2), sm(2)))
            chain.link(nc.vector.tensor_tensor(sm(2), sm(0), sm(2), ALU.mult))
            chain.link(nc.vector.tensor_tensor(sm(3), sm(2), sm(2), ALU.mult))
            terms = [1.0 / (2 * i + 1) for i in range(9)]
            chain.link(nc.vector.tensor_scalar(sm(0), sm(3), terms[8], terms[7], ALU.mult, ALU.add))
            for i in range(6, -1, -1):
                chain.link(nc.vector.tensor_tensor(sm(0), sm(0), sm(3), ALU.mult))
                chain.link(nc.vector.tensor_scalar(sm(0), sm(0), terms[i], None, ALU.add))
            chain.link(nc.vector.tensor_tensor(sm(0), sm(0), sm(2), ALU.mult))
            chain.link(nc.vector.scalar_tensor_tensor(sm(0), sm(0), 2.0, sm(1), ALU.mult, ALU.add))
            nc.vector.tensor_scalar(decay[:, 0, :, :], sm(0), -LRU_C / 2, None, ALU.mult)
            nc.vector.tensor_scalar(decay[:, 1, :, :], sm(0), LRU_C / 2, None, ALU.mult)\
                .then_inc(sp_ready, 1)

            def seam(b):
                l, trim = b // 3, b > 0 and trimmed(b - 1)
                g = ("ffn1_pre_g", "mix_pre_g", "ffn2_pre_g")[b % 3]
                if b > 0:
                    dve.wait_ge(rs_post, b)
                for k in range(DC):
                    hk, fk = toks(h[:, k, :], trim), toks(f(b - 1, k), trim) if b else None
                    if b > 0:
                        if b == NB and k >= 2:
                            dve.wait_ge(h_ready, DC * (b - 1) + k - 1)
                        step = toks(tmp[3 + (k % 2 if b == NB else 0)], trim)
                        chain.link(nc.vector.tensor_tensor(step, fk, toks(tmp[2], trim), ALU.mult))
                        nc.vector.tensor_tensor(hk, hk, step, ALU.add).then_inc(h_ready, 1)
                    if b < NB:
                        dve.wait_ge(xh_ready, DC * b + k + 1)
                        nc.vector.scalar_tensor_tensor(toks(xl[:, k, :], trim), hk, col(g, l, k),
                                                       toks(xh[:, k, :], trim).bitcast(F32),
                                                       ALU.mult, ALU.subtract).then_inc(xl_ready, 1)

            def output_sum(b):
                trim = trimmed(b)
                for m in range(1, DC - 1):
                    dve.wait_ge(sq_ready, DC * b + m + 1)
                    if m >= 2:
                        dve.wait_ge(sum_ready, NSUM * b + m - 1)
                    s = toks(tmp[4], trim)
                    nc.vector.tensor_tensor(s, s, toks(tmp[m % 2], trim), ALU.add).then_inc(sum_ready, 1)

            def ffn(b):
                s0, f0 = slot0[b], (b // 3 * 2 + b % 3 // 2) * FC
                u0, trim = U[b, "gu"], b > 0 and trimmed(b - 1)

                def hidden(m, it=0):
                    adv, mm = it * RING, m + 2 * it
                    ug, uu = u0 + 2 * m, u0 + 2 * m + 1
                    dve.wait_ge(slots_used, slot_used(s0 + 2 * m) + adv)
                    nc.vector.tensor_tensor(halves(tmp[0], trim), unit(ug, trim), halves(rs_in, trim),
                                            ALU.mult).then_inc(psum_free[pair_of(ug)], 1)
                    dve.wait_ge(slots_used, slot_used(s0 + 2 * m + 1) + adv)
                    nc.vector.tensor_tensor(halves(tmp[1], trim), unit(uu, trim), halves(rs_in, trim),
                                            ALU.mult).then_inc(psum_free[pair_of(uu)], 1)
                    dve.wait_ge(psum_free[pair_of(uu)], read_out(uu) + it)
                    dve.wait_ge(silu_ready, f0 + mm + 1)
                    nc.vector.tensor_tensor(toks(tmp[3], trim), toks(tmp[2], trim), toks(tmp[1], trim),
                                            ALU.mult).then_inc(hid_ready, 1)
                    dve.wait_ge(hidh_ready, f0 + mm + 1)
                    nc.vector.tensor_tensor(toks(hidl[:, mm, :], trim), toks(tmp[3], trim),
                                            toks(hidh[:, mm, :], trim).bitcast(F32),
                                            ALU.subtract).then_inc(hidl_ready, 1)

                dve.wait_ge(rs_pre, b + 1)
                hidden(0)
                hidden(1)
                with dve.Fori(0, FC // 2 - 1) as j:
                    hidden(2, j)
                    hidden(3, j)
                output_sum(b)

            def scaled(dst, u, n):
                dve.wait_ge(slots_used, slot_used(n))
                nc.vector.tensor_tensor(halves(dst, False), unit(u, False), halves(rs_in, False),
                                        ALU.mult).then_inc(psum_free[pair_of(u)], 1)
                dve.wait_ge(psum_free[pair_of(u)], read_out(u))

            def mixer(b):
                l, s0 = b // 3, slot0[b]
                dve.wait_ge(rs_pre, b + 1)
                dve.wait_ge(slots_used, slot_used(s0))
                nc.vector.memset(xr[:, :, 0:CONV - 1], 0.0)
                for c in range(WC):
                    scaled(xr[:, c, CONV - 1:], U[b, "xr"] + c, s0 + S_XR + c)
                    x = xc[:, c, :]
                    cw = "lru_conv_w"
                    chain.link(nc.vector.tensor_scalar(x, xr[:, c, CONV - 1:], col(cw, l, (CONV - 1) * WC + c),
                                                       col("lru_conv_b", l, c), ALU.mult, ALU.add))
                    for k in range(CONV - 1):
                        ins = nc.vector.scalar_tensor_tensor(x, xr[:, c, k:k + T], col(cw, l, k * WC + c), x,
                                                             ALU.mult, ALU.add)
                        if k < CONV - 2:
                            chain.link(ins)
                        else:
                            ins.then_inc(xc_ready, 1)
                for c in range(WC):
                    dve.wait_ge(xch_ready, WC * l + c + 1)
                    nc.vector.tensor_tensor(xcl[:, c, :], xc[:, c, :], xch[:, c, :].bitcast(F32),
                                            ALU.subtract).then_inc(xcl_ready, 1)
                square_sum(b, "cq", cq, QC, s0 + S_CQ, tmp[0], qsum_ready)
                for c in range(QC):
                    dve.wait_ge(cqh_ready, QC * l + c + 1)
                    nc.vector.scalar_tensor_tensor(cql[:, c, :], cq[:, c, :], col("mla_q_norm_g", l, c),
                                                   cqh[:, c, :].bitcast(F32), ALU.mult,
                                                   ALU.subtract).then_inc(cql_ready, 1)
                square_sum(b, "ckv", ckv, KVC, s0 + S_CKV, tmp[1], kvsum_ready)
                dve.wait_ge(decay_ready, 2 * WC * (l + 1))
                for c in range(WC):
                    chain.link(nc.vector.scalar_tensor_tensor(ig[:, c, :], ig[:, c, :], 1.0, xc[:, c, :],
                                                              ALU.add, ALU.mult))
                    chain.link(nc.vector.tensor_tensor(xc[:, c, :], av[:, c, :], av[:, c, :], ALU.mult))
                    nc.vector.scalar_tensor_tensor(rg[:, c, :], xc[:, c, :], 1.0, rg[:, c, :],
                                                   ALU.add, ALU.mult).then_inc(lru_c, 1)
                dve.wait_ge(rope1_in, 16 * (l + 1))
                kr2 = 2 * ROPE
                chain.link(nc.vector.tensor_tensor(tmp[4][0:kr2], ropet[1][0:kr2], rs_in[0:kr2], ALU.mult))
                u = U[b, "kr"]
                dve.wait_ge(slots_used, slot_used(s0 + S_KR))
                nc.vector.tensor_tensor(halves(tmp[4][0:kr2], False), unit(u, False)[0:kr2],
                                        halves(tmp[4][0:kr2], False), ALU.mult)\
                    .then_inc(psum_free[pair_of(u)], 1)
                scaled(gr[:, 0, :], U[b, "gr"], s0 + S_GR)
                dve.wait_ge(rs_kv, l + 1)
                for c in range(KVC):
                    nc.vector.tensor_tensor(ckv[:, c, :], ckv[:, c, :], tmp[3][:, :], ALU.mult)\
                        .then_inc(ckvn_ready, 1)
                for c in range(KVC):
                    dve.wait_ge(ckvh_ready, KVC * l + c + 1)
                    nc.vector.scalar_tensor_tensor(ckvl[:, c, :], ckv[:, c, :], col("mla_kv_norm_g", l, c),
                                                   ckvh[:, c, :].bitcast(F32), ALU.mult,
                                                   ALU.subtract).then_inc(ckvl_ready, 1)
                for c in range(WC):
                    if c:
                        scaled(gr[:, c, :], U[b, "gr"] + c, s0 + S_GR + c)
                    dve.wait_ge(lru_root, WC * l + c + 1)
                    chain.link(nc.vector.tensor_tensor(rg[:, c, :], rg[:, c, :], ig[:, c, :], ALU.mult))
                    nc.vector.tensor_tensor_scan(xc[:, c, :], av[:, c, :], rg[:, c, :], 0.0,
                                                 ALU.mult, ALU.add)
                dve.wait_ge(rs_q, l + 1)
                dve.wait_ge(rope0_in, 16 * (l + 1))
                for i in range(2):
                    chain.link(nc.vector.tensor_tensor(ropet[i][:, :], ropet[i][:, :], tmp[2][:, :],
                                                       ALU.mult))
                for c in range(WC):
                    dve.wait_ge(gelu_ready, WC * l + c + 1)
                    nc.vector.tensor_tensor(xc[:, c, :], xc[:, c, :], gr[:, c, :], ALU.mult)\
                        .then_inc(y_ready, 1)
                u = U[b, "sel"]
                dve.wait_ge(psum_free[pair_of(u)], read_out(u))
                for i, (p0, p1) in enumerate(((NOPE, P), (0, NOPE))):
                    nc.vector.tensor_copy(kt_of[i][p0:p1, :, :],
                                          tmp[0][p0:p1, :].unsqueeze(1).broadcast_to([NOPE, 4, T]))\
                        .then_inc(krope_ready, 1)
                for c in range(1, WC):
                    dve.wait_ge(ysq_ready, WC * l + c + 1)
                    if c > 1:
                        dve.wait_ge(lsum_ready, 3 * l + c - 1)
                    nc.vector.tensor_tensor(ig[:, 0, :], ig[:, 0, :], ig[:, c, :], ALU.add)\
                        .then_inc(lsum_ready, 1)

                def queries(hd):
                    u = unit_q(b, hd)
                    if hd % 2 == 0:
                        dve.wait_ge(q_mm, HEADS // 2 * l + hd // 2 + 1)
                    else:
                        dve.wait_ge(slots_used, slot_used(s0 + S_Q + hd // 2))
                    nc.vector.tensor_tensor(halves(qt(hd), False), unit(u, False),
                                            halves(ropet[hd % 2], False), ALU.mult)\
                        .then_inc(psum_free[pair_of(u)], 1)

                queries(0)
                queries(1)
                dve.wait_ge(rs_lru, l + 1)
                for c in range(WC):
                    nc.vector.tensor_tensor(xc[:, c, :], xc[:, c, :], tmp[4][:, :], ALU.mult)\
                        .then_inc(yn_ready, 1)
                queries(2)
                queries(3)
                for c in range(WC):
                    dve.wait_ge(ylh_ready, WC * l + c + 1)
                    nc.vector.scalar_tensor_tensor(yll[:, c, :], xc[:, c, :], col("lru_out_g", l, c),
                                                   ylh[:, c, :].bitcast(F32), ALU.mult,
                                                   ALU.subtract).then_inc(yll_ready, 1)
                for hd in range(4, HEADS):
                    queries(hd)

                if not trimmed(b):
                    m0 = n_meta_layers(l)
                    nm = N_META
                    s0p = pair(0)[0:nm, 0:P].rearrange("p (h k) -> p h k", h=HEADS)
                    p0 = prob[0][0:nm, 0:P].rearrange("p (h k) -> p h k", h=HEADS)
                    mx, dn = small[0:nm, 40:48], small[0:nm, 48:56]
                    dve.wait_ge(s0_mm, m0 + 1)
                    nc.vector.tensor_reduce(mx, s0p, AX.X, ALU.max).then_inc(s0_max, 1)
                    dve.wait_ge(s0_max, 2 * m0 + 1)
                    nc.vector.tensor_tensor(p0, s0p, mx.unsqueeze(2).broadcast_to([nm, HEADS, nm]),
                                            ALU.subtract).then_inc(s0_max, 1)
                    dve.wait_ge(s0_exp, m0 + 1)
                    chain.link(nc.vector.tensor_reduce(dn, p0, AX.X, ALU.add))
                    chain.link(nc.vector.reciprocal(dn, dn))
                    dve.wait_ge(t0_mm, m0 + 1)
                    nc.vector.tensor_copy(probT[0][0:nm, 0:P], pair(1)[0:nm, 0:P]).then_inc(t0_copied, 1)
                    dve.wait_ge(o0_mm, m0 + 1)
                    nc.vector.tensor_tensor(
                        osb0[0:nm, :].rearrange("p (h d) -> p h d", h=HEADS),
                        pair(2)[0:nm, 0:512].rearrange("p (h d) -> p h d", h=HEADS),
                        dn.unsqueeze(2).broadcast_to([nm, HEADS, VD]), ALU.mult).then_inc(t0_copied, 1)

                def head_out(hd):
                    H = HEADS * l + hd
                    rd = small[:, 56:60]
                    dve.wait_ge(pv_mm, ITEMS * l + NQ * (hd + 1))
                    chain.link(nc.vector.reciprocal(rd, small[:, 16 + NQ * (hd % 2):20 + NQ * (hd % 2)]))
                    nc.vector.tensor_tensor(
                        osb[:, :, hd * VD:(hd + 1) * VD],
                        pair(3)[:, (hd % 2) * 512:(hd % 2) * 512 + NQ * VD].rearrange("p (i d) -> p i d", i=NQ),
                        rd.unsqueeze(2).broadcast_to([P, NQ, VD]), ALU.mult).then_inc(o_copied, 1)

                for e in range(ITEMS + 2):
                    if e < ITEMS:
                        E, i = ITEMS * l + e, e % NQ + 1
                        nk, pr = keys_of(i), pair(e % 3)
                        dve.wait_ge(s_mm, E + 1)
                        if e >= 4:
                            dve.wait_ge(prob_ready, E - 3)
                        src = (pr[:, 0:nk] if i < NQ else
                               pr.rearrange("p (a b) -> p a b", a=2)[:, :, 0:HALF])
                        nc.vector.tensor_reduce(small[:, 8 + e % 4:9 + e % 4], src,
                                                AX.X if i < NQ else AX.XY, ALU.max,
                                                negate=True).then_inc(max_ready, 1)
                    if 1 <= e <= ITEMS and not copied_by_act((e - 1) % NQ + 1):
                        q = e - 1
                        Q, i = ITEMS * l + q, q % NQ + 1
                        dve.wait_ge(t_mm, Q + 1)
                        if q >= 3:
                            dve.wait_ge(pv_mm, Q - 2)
                        nc.vector.tensor_copy(probT[q % 3][:, 0:(i + 1) * P], pair(q % 3)[:, 0:(i + 1) * P])\
                            .then_inc(t_dve, 1)
                    if e >= 2 and (e - 2) % NQ == NQ - 1:
                        head_out((e - 2) // NQ)
                dve.wait_ge(rs_att, l + 1)
                if not trimmed(b):
                    nc.vector.tensor_scalar(osb0[0:N_META, :], osb0[0:N_META, :], small[0:N_META, 36:37],
                                            None, ALU.mult).then_inc(on_ready, 1)
                for i in range(NQ):
                    nc.vector.tensor_scalar(osb[:, i, :], osb[:, i, :], small[:, 32 + i:33 + i],
                                            None, ALU.mult).then_inc(on_ready, 1)
                for c in range(WC):
                    dve.wait_ge(yah_ready, WC * l + c + 1)
                    u = U[b, "tr"] + c
                    pr, g = pair(pair_of(u)), col("mla_out_g", l, c)
                    if not trimmed(b):
                        nc.vector.scalar_tensor_tensor(xl[:, WC + c, 0:N_META], pr[:, 512:512 + N_META], g,
                                                       xh[:, WC + c, 0:N_META].bitcast(F32), ALU.mult,
                                                       ALU.subtract)
                    nc.vector.scalar_tensor_tensor(xl[:, WC + c, N_META:T], pr[:, 0:SEQ], g,
                                                   xh[:, WC + c, N_META:T].bitcast(F32), ALU.mult,
                                                   ALU.subtract).then_inc(psum_free[pair_of(u)], 1)
                output_sum(b)

            def square_sum(b, name, z, nch, n0, acc, done):
                for c in range(nch):
                    scaled(z[:, c, :], U[b, name] + c, n0 + c)
                    if c == 0:
                        chain.link(nc.vector.tensor_tensor(acc[:, :], z[:, c, :], z[:, c, :], ALU.mult))
                    else:
                        chain.link(nc.vector.tensor_tensor(tmp[4][:, :], z[:, c, :], z[:, c, :], ALU.mult))
                        ins = nc.vector.tensor_tensor(acc[:, :], acc[:, :], tmp[4][:, :], ALU.add)
                        if c == nch - 1:
                            ins.then_inc(done, 1)
                        else:
                            chain.link(ins)

            for b in range(NB):
                seam(b)
                if b % 3 == 1:
                    mixer(b)
                else:
                    ffn(b)
            seam(NB)

        @block.tensor
        def _(pe):
            pe.sem_inc(slots_used, RING)
            for i in range(4):
                pe.sem_inc(psum_free[i], 1)

            def mm(o, w, x, start, stop):
                return nc.tensor.matmul(o, w, x, start=start, stop=stop)

            def tile(u, n, t, xhk, xlk, grp, first, last):
                pr, r = pair(pair_of(u)), n % RING
                wh, wl = whi[:, r, t * P:(t + 1) * P], wlo[:, r, t * P:(t + 1) * P]
                for w, x, start, stop in ((wh, xhk, first, False), (wh, xlk, False, False),
                                          (wl, xhk, False, last)):
                    for t0, nt, c0 in grp:
                        ins = mm(pr[:, c0:c0 + nt], w, x[:, t0:t0 + nt], start, stop)
                return ins

            def slot_in(n, adv=0):
                pe.wait_ge(lo_ready, n + 1 + adv)

            def unit_free(u, it=0):
                pe.wait_ge(psum_free[pair_of(u)], free_for(u) + it)

            def product(u, n, trim, x=None, adv=0, it=0):
                x = x or [(xh[:, k, :], xl[:, k, :]) for k in range(DC)]
                slot_in(n, adv)
                unit_free(u, it)
                for k in range(DC):
                    ins = tile(u, n, k, x[k][0], x[k][1], groups(trim), k == 0, k == DC - 1)
                ins.then_inc(slots_used, 1)

            def first_two(b, u, n, trim):
                for q in range(2):
                    slot_in(n + q)
                    unit_free(u + q)
                for k in range(DC):
                    pe.wait_ge(xl_ready, DC * b + k + 1)
                    for q in range(2):
                        ins = tile(u + q, n + q, k, xh[:, k, :], xl[:, k, :], groups(trim),
                                   k == 0, k == DC - 1)
                        if k == DC - 1:
                            ins.then_inc(slots_used, 1)

            def partition_sum(u, trim, srcs, s):
                unit_free(u)
                for i, src in enumerate(srcs):
                    for t0, nt, c0 in groups(trim):
                        ins = mm(pair(pair_of(u))[:, c0:c0 + nt], ones, src[:, t0:t0 + nt],
                                 i == 0, i == len(srcs) - 1)
                ins.then_inc(s, 1)

            def stat_in(b):
                trim = b > 0 and trimmed(b - 1)
                pe.wait_ge(hsum_ready, NHSUM * (b + 1))
                partition_sum(U[b, "pre"], trim, [tmp[4]], stat_pre)

            def stat_out(b):
                trim = trimmed(b)
                pe.wait_ge(sum_ready, NSUM * (b + 1))
                pe.wait_ge(sq_ready, DC * (b + 1))
                partition_sum(U[b + 1, "post"], trim, [tmp[4], tmp[(DC - 1) % 2]], stat_post)

            def ffn(b):
                s0, f0 = slot0[b], (b // 3 * 2 + b % 3 // 2) * FC
                u0, ud, tin, tout = U[b, "gu"], U[b, "out"], b > 0 and trimmed(b - 1), trimmed(b)
                first_two(b, u0, s0, tin)
                stat_in(b)
                product(u0 + 2, s0 + 2, tin)
                product(u0 + 3, s0 + 3, tin)
                with pe.Fori(0, FC // 2 - 1) as j:
                    for m in range(4):
                        product(u0 + 4 + m, s0 + 4 + m, tin, adv=j * RING, it=j)

                with pe.Fori(0, 2) as j:
                    for m in range(4):
                        unit_free(ud + m, j)
                        for q in range(2):
                            n = s0 + 2 * FC + 2 * m + q
                            slot_in(n, j * 8)
                            pe.wait_ge(hidl_ready, f0 + FH * (q + 1))
                            for t in range(FH):
                                k = FH * q + t
                                ins = tile(ud + m, n, t, hidh[:, k, :], hidl[:, k, :], groups(tout),
                                           k == 0, k == FC - 1)
                            ins.then_inc(slots_used, 1)

            def mixer(b):
                l, s0 = b // 3, slot0[b]
                grp = groups(False)
                first_two(b, U[b, "xr"], s0, False)
                stat_in(b)
                for c in range(2, WC):
                    product(U[b, "xr"] + c, s0 + S_XR + c, False)
                for c in range(QC):
                    product(U[b, "cq"] + c, s0 + S_CQ + c, False)
                n = s0 + S_GATE
                slot_in(n)
                if l == 0:
                    pe.wait_ge(sp_ready, 1)
                for g in range(2 * WC):
                    u, c = U[b, "gate"] + g, g % WC
                    if g < WC:
                        pe.wait_ge(xcl_ready, WC * l + c + 1)
                    unit_free(u)
                    ins = tile(u, n, g, xch[:, c, :], xcl[:, c, :], grp, True, True)
                    ins.then_inc(gate_mm if g < 2 * WC - 1 else slots_used, 1)
                for c in range(KVC):
                    product(U[b, "ckv"] + c, s0 + S_CKV + c, False)
                pe.wait_ge(qsum_ready, l + 1)
                partition_sum(U[b, "statq"], False, [tmp[0]], stat_mix)
                product(U[b, "kr"], s0 + S_KR, False)
                pe.wait_ge(kvsum_ready, l + 1)
                partition_sum(U[b, "statkv"], False, [tmp[1]], stat_mix)
                product(U[b, "gr"], s0 + S_GR, False)
                for c in range(1, WC):
                    product(U[b, "gr"] + c, s0 + S_GR + c, False)
                u = U[b, "sel"]
                unit_free(u)
                ukr = U[b, "kr"]
                pe.wait_ge(psum_free[pair_of(ukr)], read_out(ukr))
                for t0, nt, c0 in grp:
                    ins = mm(pair(pair_of(u))[:, c0:c0 + nt], sel[0:2 * ROPE], tmp[4][0:2 * ROPE, t0:t0 + nt],
                             True, True)
                ins.then_inc(sel_mm, 1)
                n = s0 + S_V
                slot_in(n)
                pe.wait_ge(ckvl_ready, KVC * (l + 1))
                r = n % RING
                for i in range(3):
                    u = U[b, "v"] + i
                    unit_free(u)
                    for q in range(2 if i < 2 else 1):
                        t0 = block_of(2 * i + q)[0]
                        o = pair(pair_of(u))[:, q * 512:(q + 1) * 512]
                        for c in range(KVC):
                            wv = slice(c * W, (c + 1) * W)
                            mm(o, ckvh[:, c, t0:t0 + P], whi[:, r, wv], c == 0, False)
                            mm(o, ckvh[:, c, t0:t0 + P], wlo[:, r, wv], False, False)
                            ins = mm(o, ckvl[:, c, t0:t0 + P], whi[:, r, wv], False, c == KVC - 1)
                    ins.then_inc(v_mm if i < 2 else slots_used, 1)
                n = s0 + S_K
                slot_in(n)
                for i in range(HEADS // 2):
                    u = U[b, "k"] + i
                    unit_free(u)
                    for c in range(KVC):
                        ins = tile(u, n, KVC * i + c, ckvh[:, c, :], ckvl[:, c, :], grp, c == 0, c == KVC - 1)
                    ins.then_inc(k_mm if i < HEADS // 2 - 1 else slots_used, 1)
                pe.wait_ge(cql_ready, QC * (l + 1))
                for hd in range(HEADS):
                    u, n = unit_q(b, hd), s0 + S_Q + hd // 2
                    if hd % 2 == 0:
                        slot_in(n)
                    unit_free(u)
                    for c in range(QC):
                        ins = tile(u, n, QC * (hd % 2) + c, cqh[:, c, :], cql[:, c, :], grp,
                                   c == 0, c == QC - 1)
                    ins.then_inc(slots_used if hd % 2 else q_mm, 1)
                    if hd == 1:
                        pe.wait_ge(lsum_ready, 3 * (l + 1))
                        us = U[b, "statl"]
                        partition_sum(us, False, [ig[:, 0, :]], stat_mix)
                attention(b)
                ot = U[b, "tr"]
                n_on = NQ * (l + 1) + n_meta_layers(l) + (0 if trimmed(b) else 1)
                pe.wait_ge(on_ready, n_on)
                for c in range(WC):
                    u = ot + c
                    unit_free(u)
                    pr = pair(pair_of(u))
                    if not trimmed(b):
                        nc.tensor.transpose(pr[:, 512:512 + N_META], osb0[0:N_META, c * P:(c + 1) * P],
                                            ident[0:N_META, 0:N_META])
                    for i in range(NQ):
                        ins = nc.tensor.transpose(pr[:, i * P:(i + 1) * P], osb[:, i, c * P:(c + 1) * P], ident)
                    ins.then_inc(tr_mm, 1)
                pe.wait_ge(yll_ready, WC * (l + 1))
                for c in range(WC):
                    pe.wait_ge(psum_free[pair_of(ot + c)], read_out(ot + c))
                x = [(ylh[:, k, :], yll[:, k, :]) for k in range(WC)] + \
                    [(xh[:, k, :], xl[:, k, :]) for k in range(WC, DC)]
                with pe.Fori(0, DC // 4) as j:
                    for m in range(4):
                        product(U[b, "out"] + m, s0 + S_OUT + m, trimmed(b), x=x, adv=j * RING, it=j)

            def attention(b):
                l = b // 3
                last = U[b, "tr"] - 1
                for u in range(last - 3, last + 1):
                    pe.wait_ge(psum_free[pair_of(u)], read_out(u))
                pe.wait_ge(krope_ready, 2 * (l + 1))
                if not trimmed(b):
                    m0, nm = n_meta_layers(l), N_META
                    for hd in range(HEADS):
                        o = pair(0)[0:nm, hd * nm:(hd + 1) * nm]
                        mm(o, qt(hd)[:, 0:nm], kt(hd)[:, 0:nm], True, False)
                        ins = mm(o, identb[0:nm, 0:nm], maskb[0:nm, 0:nm], False, True)
                    ins.then_inc(s0_mm, 1)
                    pe.wait_ge(s0_exp, m0 + 1)
                    for hd in range(HEADS):
                        ins = mm(pair(1)[0:nm, hd * nm:(hd + 1) * nm], prob[0][0:nm, hd * nm:(hd + 1) * nm],
                                 ident[0:nm, 0:nm], True, True)
                    ins.then_inc(t0_mm, 1)
                    pe.wait_ge(t0_copied, 2 * m0 + 1)
                    for hd in range(HEADS):
                        ins = mm(pair(2)[0:nm, hd * VD:(hd + 1) * VD], probT[0][0:nm, hd * nm:(hd + 1) * nm],
                                 vt[0:nm, 0, hd * VD:(hd + 1) * VD], True, True)
                    ins.then_inc(o0_mm, 1)
                    pe.wait_ge(t0_copied, 2 * m0 + 2)

                def scores(e):
                    E, hd, i = ITEMS * l + e, e // NQ, e % NQ + 1
                    t0, nk, pr = block_of(i)[0], keys_of(i), pair(e % 3)
                    if e >= 3:
                        copied(e - 3)
                    parts = [(0, nk, 0)] if i < NQ else [(0, HALF, 0), (HALF, HALF, 512)]
                    for k0, n, c0 in parts:
                        tail = k0 + n == nk
                        mm(pr[:, c0:c0 + n], qt(hd)[:, t0:t0 + P], kt(hd)[:, k0:k0 + n], True, not tail)
                        if tail:
                            ins = mm(pr[:, c0 + n - P:c0 + n], identb[:, :], maskb[:, :], False, True)
                    ins.then_inc(s_mm, 1)

                def copied(e):
                    full, i = ITEMS // 2 * l + e // NQ * 2, e % NQ + 1
                    if copied_by_act(i):
                        pe.wait_ge(t_act, full + i)
                    else:
                        pe.wait_ge(t_dve, full + i - 2)

                def transposes(e):
                    E, i = ITEMS * l + e, e % NQ + 1
                    pe.wait_ge(prob_ready, E + 1)
                    for j in range(i + 1):
                        k0 = block_of(j)[0]
                        ins = nc.tensor.transpose(pair(e % 3)[:, j * P:(j + 1) * P],
                                                  prob[e % 3][:, k0:k0 + P], ident)
                    ins.then_inc(t_mm, 1)

                def outputs(e):
                    hd, i = e // NQ, e % NQ + 1
                    copied(e)
                    if i == 1 and hd >= 2:
                        pe.wait_ge(o_copied, HEADS * l + hd - 1)
                    c0 = (hd % 2) * 512 + (i - 1) * VD
                    for j in range(i + 1):
                        kn = block_of(j)[1]
                        ins = mm(pair(3)[:, c0:c0 + VD], probT[e % 3][0:kn, j * P:(j + 1) * P],
                                 vt[0:kn, j, hd * VD:(hd + 1) * VD], j == 0, j == i)
                    ins.then_inc(pv_mm, 1)

                for e in range(ITEMS + 2):
                    if e < ITEMS:
                        scores(e)
                    if 1 <= e <= ITEMS:
                        transposes(e - 1)
                    if e >= 2:
                        outputs(e - 2)
                pe.wait_ge(o_copied, HEADS * (l + 1))

            for b in range(NB):
                if b == 0:
                    pe.wait_ge(consts_in, 32)
                if b % 3 == 1:
                    mixer(b)
                else:
                    ffn(b)
                stat_out(b)


def _feature_columns(v):
    v = v.reshape(v.shape[0], -1, P)
    return v.transpose(0, 2, 1)


def _tiles(w, rows, cols):
    return w.reshape(w.shape[0], rows, P, cols, P).transpose(0, 3, 2, 1, 4).reshape(w.shape[0], cols, P, rows * P)


def _block_diagonal(w):
    L, H, n, _ = w.shape
    o = np.zeros((L, P, H // 2, P), w.dtype)
    for h in range(H):
        s = (h % 2) * n
        o[:, s:s + n, h // 2, s:s + n] = w[:, h]
    return o


def _swap(w):
    n = ROPE // 2
    return np.concatenate([w[..., n:], w[..., :n]], axis=-1)


def _consts():
    c = np.zeros((P, NCONST), np.float32)
    c[:, C_ID:C_ID + P] = np.eye(P)
    c[:, C_ONE:C_ONE + P] = 1.0
    for i in range(ROPE):
        for q in range(P // ROPE):
            c[i, C_SEL + q * ROPE + i] = 1.0
            c[ROPE + i, C_SEL + q * ROPE + i] = 1.0
    c[:, C_MASK:C_MASK + P] = np.triu(np.full((P, P), MASKED), 1)
    c[:, C_EPS] = EPS
    c[:, C_LNS] = -0.5 * np.log(NOPE + ROPE)
    return c


def _rope():
    inv = (1.0 / (np.float32(ROPE_THETA) ** (np.arange(0, ROPE, 2, dtype=np.float32) / np.float32(ROPE))))
    ang = np.arange(T, dtype=np.float32)[None, :] * inv.astype(np.float32)[:, None]
    cos, sin = np.cos(ang), np.sin(ang)
    factors = np.concatenate([cos, cos, -sin, sin], axis=0)
    one = np.ones((NOPE, T))
    return np.stack([np.concatenate([one, factors]), np.concatenate([factors, one])]).astype(np.float32)


def kernel(**inputs):
    import concourse.bacc as bacc
    from concourse.bass_utils import run_bass_kernel_spmd

    g = {k: np.asarray(v) for k, v in inputs.items()}
    depth, d_ff = g["ffn1_w_gate"].shape[0], g["ffn1_w_gate"].shape[2]
    FC = d_ff // P
    arrays = {"consts": _consts(), "rope": _rope()}
    x = np.concatenate([g["meta_tokens"], g["x"][0]], axis=0)
    arrays["x"] = x.T.reshape(DC, P, T)
    arrays["params"] = np.concatenate([_feature_columns(g[n]) for n, _ in PARAMS], axis=2).transpose(1, 0, 2)
    for f in ("ffn1", "ffn2"):
        arrays[f + "_gate"] = _tiles(g[f + "_w_gate"], DC, FC)
        arrays[f + "_up"] = _tiles(g[f + "_w_up"], DC, FC)
        arrays[f + "_down"] = _tiles(g[f + "_w_down"], FC, DC).reshape(depth, DC, P, 2, FC // 2 * P)\
            .transpose(0, 1, 3, 2, 4)
    w = g["w_in"]
    kr = w[:, :, 2 * W + QL + KVL:]
    w = np.concatenate([w[:, :, 0:W], w[:, :, 2 * W:2 * W + QL + KVL], kr, _swap(kr), kr, _swap(kr),
                        w[:, :, W:2 * W]], axis=2)
    arrays["w_in"] = _tiles(w, DC, w.shape[2] // P)
    arrays["w_gates"] = np.concatenate([_block_diagonal(g["lru_w_a"]), _block_diagonal(g["lru_w_x"])],
                                       axis=2).reshape(depth, P, 2 * WC * P)
    q = g["mla_w_uq"].reshape(depth, QL, HEADS, NOPE + ROPE)
    nope, rope = q[..., :NOPE], q[..., NOPE:]
    even = np.concatenate([nope, rope, _swap(rope)], axis=-1)
    odd = np.concatenate([rope, _swap(rope), nope], axis=-1)
    q = np.stack([even[:, :, 0::2], odd[:, :, 1::2]], axis=3).reshape(depth, QL, HEADS * P)
    arrays["w_q"] = _tiles(q, QC, HEADS).reshape(depth, HEADS // 2, 2, P, QC * P)\
        .transpose(0, 1, 3, 2, 4).reshape(depth, HEADS // 2, P, 2 * QC * P)
    kv = g["mla_w_ukv"].reshape(depth, KVL, HEADS, NOPE + VD)
    k = kv[..., :NOPE].reshape(depth, KVL, HEADS * NOPE)
    v = kv[..., NOPE:].reshape(depth, KVL, HEADS * VD)
    arrays["w_k"] = _tiles(k, KVC, HEADS // 2).transpose(0, 2, 1, 3).reshape(depth, P, -1)
    arrays["w_v"] = v.reshape(depth, KVC, P, W).transpose(0, 2, 1, 3).reshape(depth, P, -1)
    arrays["w_out"] = _tiles(g["w_out"], DC, DC)

    nc = bacc.Bacc("TRN2", target_bir_lowering=False, num_devices=1, dynamic_dma_scratch_size=64)
    arrays = {f"in_{n}": np.ascontiguousarray(v) for n, v in arrays.items()}
    a = {n[3:]: nc.dram_tensor(n, v.shape, mybir.dt.from_np(v.dtype), kind="ExternalInput").ap()
         for n, v in arrays.items()}
    out = nc.dram_tensor("out_t", (DC, P, SEQ), F32, kind="ExternalOutput").ap()
    build_program(nc, a, out, depth, d_ff)
    r = run_bass_kernel_spmd(nc, [arrays], core_ids=[0])
    o = r.results[0]["out_t"]
    return np.ascontiguousarray(o.reshape(D, SEQ).T)[None]
```

```python
from contextlib import ExitStack

import numpy as np

import concourse.bass as bass
from concourse import mybir

F32 = mybir.dt.float32
F32R = mybir.dt.float32r
BF16 = mybir.dt.bfloat16
ALU = mybir.AluOpType
ACT = mybir.ActivationFunctionType
AX = mybir.AxisListType

P = 128
EPS = 1e-6
LRU_C = 8.0
N_META = 16
SEQ = 512
T = N_META + SEQ
HALF = T // 2
D = 1024
DC = D // P
CONV = 4
W = 512
WC = W // P
HEADS = 8
NOPE = 64
ROPE = 32
VD = 64
QL = 384
QC = QL // P
KVL = 256
KVC = KVL // P
ROPE_THETA = 10000.0
RING = 4
MASKED = -1e30

PARAMS = [
    ("ffn1_pre_g", DC), ("ffn1_post_g", DC), ("mix_pre_g", DC), ("mix_post_g", DC),
    ("ffn2_pre_g", DC), ("ffn2_post_g", DC), ("lru_conv_w", CONV * WC), ("lru_conv_b", WC),
    ("lru_b_a", WC), ("lru_b_x", WC), ("lru_lambda", WC), ("mla_q_norm_g", QC),
    ("mla_kv_norm_g", KVC), ("lru_out_g", WC), ("mla_out_g", WC),
]
PCOL = {}
NPAR = 0
for _name, _n in PARAMS:
    PCOL[_name] = NPAR
    NPAR += _n

C_ID, C_ONE, C_SEL, C_MASK, C_EPS, C_LNS, NCONST = 0, P, 2 * P, 3 * P, 4 * P, 4 * P + 1, 4 * P + 2

S_XR, S_CQ, S_GATE, S_CKV, S_KR, S_GR, S_V, S_K, S_Q, S_OUT = 0, 4, 7, 8, 10, 11, 15, 16, 17, 21
MIX_TILES = [DC] * 7 + [2 * WC] + [DC] * 7 + [KVC * 4] + [4 * KVC] + [2 * QC] * 4 + [DC] * DC

EXP_TANH_TABLES, LN_EXP_TABLES, SILU_TABLES = 0, 6, 18

WARM_UP = 72

ACT_ORDER = {
    0: {(0, 0): [("hi", 0)], (0, 3): [("hi", 1)], (0, 8): [("hi", 2)], (1, 1): [("hi", 3)],
        (1, 4): [("pre", 0)]},
    2: {(0, 1): [("out", 6)], (0, 2): [("hi", 0)], (0, 4): [("hi", 1)], (0, 8): [("hi", 2), ("out", 7)],
        (1, 1): [("hi", 3)], (1, 3): [("pre", 0)]},
    3: {(-1, 6): [("hi", 0)], (0, 0): [("out", 5)], (0, 3): [("out", 6)], (0, 4): [("hi", 1)],
        (0, 7): [("out", 7)], (0, 8): [("hi", 2)], (1, 1): [("hi", 3)], (1, 3): [("pre", 0)]},
}
POOL_ORDER = {0: {(0, 1): (0,), (0, 3): (1,), (0, 6): (2,), (1, 3): (3,)},
              2: {(0, 3): (0,), (0, 5): (1,), (0, 6): (2,), (1, 3): (3,)},
              3: {(0, 1): (0,), (0, 4): (1,), (0, 7): (2,), (1, 3): (3,)}}


def build_program(nc, a, out, depth, d_ff):
    FC = d_ff // P
    FH = FC // 2
    MAXT = max(FH, DC)
    NB = 3 * depth
    assert FC % 2 == 0 and FC >= 6

    tiles = []
    slot0 = []
    for b in range(NB):
        slot0.append(len(tiles))
        tiles += MIX_TILES if b % 3 == 1 else [DC] * (2 * FC) + [FH] * (2 * DC)
    NSLOT = len(tiles)
    MIX_UNITS = dict(xr=WC, cq=QC, gate=2 * WC, ckv=KVC, statq=1, kr=1, statkv=1, gr=WC, sel=1,
                     v=3, k=4, qa=HEADS // 2, statl=1, qb=HEADS // 2, tr=WC, out=DC)
    U = {}
    n = 0
    for b in range(NB):
        if b:
            U[b, "post"] = n
            n += 1
        U[b, "pre"] = n
        n += 1
        parts = MIX_UNITS if b % 3 == 1 else dict(gu=2 * FC, out=DC)
        for name, k in parts.items():
            U[b, name] = n
            n += k
    U[NB, "post"] = n

    def trimmed(b):
        return b >= NB - 2

    def unit_q(b, hd):
        return U[b, "qa"] + hd if hd < HEADS // 2 else U[b, "qb"] + hd - HEADS // 2

    def pair_of(u):
        return u % 4

    def free_for(u):
        return u // 4 + 1

    def read_out(u):
        return u // 4 + 2

    def slot_used(n):
        return n + 1 + RING

    split = [3 if b % 3 == 1 else 2 for b in range(NB)]

    def events(b, m, s, lead):
        last = DC - 1 - lead
        per = [last + 1 - lead + (k - lead) for k in split]
        first = DC - split[b]
        if m < first:
            return sum(per[:b]) + m + 1 - lead
        return sum(per[:b]) + first - lead + s * (split[b] - lead) + m - first + 1

    def sq_n(b, m, s=1):
        return events(b, m, s, 0)

    def sum_n(b, m, s=1):
        return events(b, m, s, 1)

    def out_slot(b, m):
        return slot0[b] + (S_OUT + m if b % 3 == 1 else 2 * FC + 2 * m + 1)

    def half_n(b, m):
        return sum(split[:b]) + m - (DC - split[b]) + 1

    def seam_n(b, s, k):
        return 2 * DC * b + DC * s + k + 1

    def hsum_n(b, s, k):
        return 2 * (DC - 1) * b + (DC - 1) * s + k

    with ExitStack() as ctx:
        def sem(name):
            return ctx.enter_context(nc.semaphore(name))

        base = [(nc.sbuf_base + 31) // 32 * 32]

        def sb_at(name, offset, shape, dt):
            return nc.alloc_sbuf_tensor_at(name, shape, dt, offset=offset)

        def sb(name, shape, dt):
            size = 2 if dt == BF16 else 4
            for s in shape[1:]:
                size *= s
            t = sb_at(name, base[0], shape, dt)
            base[0] += (size + 31) // 32 * 32
            return t

        CH = T * 4
        h = sb("h", [P, DC, T], F32)
        xh_at = base[0]
        xh = sb("xh", [P, DC, T], F32R)
        xl_at = base[0]
        xl = sb("xl", [P, DC, T], F32R)
        f_ffn = sb_at("f_ffn", xl_at, [P, DC, T], F32)
        raw = sb("raw", [P, RING, MAXT * P], F32)
        whi = sb("whi", [P, RING, MAXT * P], F32R)
        wlo = sb("wlo", [P, RING, MAXT * P], F32R)
        par = sb("par", [P, depth, NPAR], F32)
        half_g = sb("half_g", [P, depth, 2, DC], F32)
        half_b = sb("half_b", [P, depth, 2, WC], F32)
        decay = sb("decay", [P, 2, depth, WC], F32)
        consts = sb("consts", [P, NCONST], F32)
        identb = sb("identb", [P, P], BF16)
        maskb = sb("maskb", [P, P], BF16)
        rs_in = sb("rs_in", [P, T], F32)
        tmp = [sb(f"tmp{i}", [P, T], F32) for i in range(5)]
        small = sb("small", [P, 64], F32)
        arena = base[0]

        hidh = sb_at("hidh", arena, [P, FC, T], F32R)
        hidl = sb_at("hidl", arena + FC * CH, [P, FC, T], F32R)
        off = [arena]

        def over(name, shape, dt, at=None):
            t = sb_at(name, off[0] if at is None else at, shape, dt)
            if at is None:
                size = 4
                for s in shape[1:]:
                    size *= s
                off[0] += (size + 31) // 32 * 32
            return t

        xr_at = off[0]
        xr = over("xr", [P, WC, T + CONV - 1], F32)
        rg = over("rg", [P, WC, T], F32, xr_at)
        ylh = over("ylh", [P, WC, T], F32R, xr_at)
        gr_at = off[0]
        gr = over("gr", [P, WC, T], F32)
        xc = over("xc", [P, WC, T], F32)
        xch_at = off[0]
        xch = over("xch", [P, WC, T], F32R)
        xcl = over("xcl", [P, WC, T], F32R)
        vt = over("vt", [P, 5, HEADS * VD], F32, xch_at)
        ig_at = off[0]
        ig = over("ig", [P, WC, T], F32)
        av_at = off[0]
        av = over("av", [P, WC, T], F32)
        yll = over("yll", [P, WC, T], F32R, av_at)
        cq_at = off[0]
        cqh = over("cqh", [P, QC, T], F32R)
        cql = over("cql", [P, QC, T], F32R)
        osb = over("osb", [P, 4, HEADS * VD], F32, cq_at)
        osb0 = over("osb0", [P, HEADS * VD], F32, cq_at + 4 * HEADS * VD * 4)
        z_at = off[0]
        cq = over("cq", [P, QC, T], F32)
        ckv = over("ckv", [P, KVC, T], F32)
        ckvh = over("ckvh", [P, KVC, T], F32R)
        ckvl = over("ckvl", [P, KVC, T], F32R)
        assert 4 * HEADS * VD * 4 + HEADS * VD * 4 <= 2 * QC * CH
        prob = [over(f"prob{i}", [P, T], F32, z_at + c * CH) for i, c in enumerate((0, 1, 3))]
        probT = [over(f"probT{i}", [P, 5 * P], F32, z_at + 4 * CH + i * 5 * P * 4) for i in range(3)]
        prob.append(over("prob3", [P, T], F32, z_at + 4 * CH + 3 * 5 * P * 4))
        assert 5 * CH + 3 * 5 * P * 4 <= (QC + 3 * KVC) * CH
        ropet = [over("ropet0", [P, T], F32, z_at + 2 * CH), over("ropet1", [P, T], F32)]
        kt_of = [sb_at(f"kt{i}", at, [P, 4, T], F32) for i, at in enumerate((xh_at, xl_at))]
        qt_of = [sb_at(f"qt{i}", at + 4 * CH, [P, 4, T], F32) for i, at in enumerate((xh_at, xl_at))]
        f_mix = [sb_at(f"f_mix{i}", at, [P, WC, T], F32) for i, at in enumerate((gr_at, ig_at))]
        end = max(off[0], arena + 2 * FC * CH)
        assert end <= nc.sbuf_usable_end, end

        def kt(hd):
            return kt_of[hd % 2][:, hd // 2, :]

        def qt(hd):
            return qt_of[hd % 2][:, hd // 2, :]

        def f(b, k):
            return f_mix[k // WC][:, k % WC, :] if b % 3 == 1 else f_ffn[:, k, :]

        ps = ctx.enter_context(nc.psum_tensor("ps", [P, 8 * 512], F32))

        def pair(i):
            return ps[:, i * 1024:(i + 1) * 1024]

        ident = consts[:, C_ID:C_ID + P]
        ones = consts[:, C_ONE:C_ONE + P]
        sel = consts[:, C_SEL:C_SEL + P]
        eps = consts[:, C_EPS:C_EPS + 1]
        ln_scale = consts[:, C_LNS:C_LNS + 1]

        def col(name, l, k, p=P):
            c = PCOL[name] + k
            return par[0:p, l, c:c + 1]

        def toks(t2, trim):
            return t2[:, N_META:T] if trim else t2[:, 0:T]

        def span(trim, s):
            return (N_META + s * (SEQ // 2), SEQ // 2) if trim else (s * HALF, HALF)

        def half(t2, trim, s):
            t0, nt = span(trim, s)
            return t2[:, t0:t0 + nt]

        SQUARES = (4, 2)

        def square_of(k, s, trim):
            i = (k - 1) % SQUARES[s]
            if k == 0:
                return half(tmp[4], trim, s)
            if i < 2:
                return half(tmp[i], trim, s)
            return rs_in[:, (i - 2) * HALF:(i - 2) * HALF + span(trim, s)[1]]

        def bank(u, trim, s):
            c0 = pair_of(u) * 1024 + s * 512
            return ps[:, c0:c0 + span(trim, s)[1]]

        def halves(t2, trim):
            return toks(t2, trim).rearrange("p (a b) -> p a b", a=2)

        def unit(u, trim):
            return pair(pair_of(u)).rearrange("p (a b) -> p a b", a=2)[:, :, 0:span(trim, 0)[1]]

        def groups(trim):
            return [span(trim, s) + (512 * s,) for s in range(2)]

        consts_in = sem("consts_in")
        par_in = sem("par_in")
        zeros_ready = sem("zeros_ready")
        H_PARTS = ((0, 0, 4), (0, 4, 4), (1, 0, 8))
        h_in = [sem(f"h_in{i}") for i in range(len(H_PARTS))]
        rope0_in = sem("rope0_in")
        rope1_in = sem("rope1_in")
        raw_full = [sem(f"raw_full{i}") for i in range(RING)]
        hi_ready = sem("hi_ready")
        lo_ready = sem("lo_ready")
        slots_used = sem("slots_used")
        psum_free = [sem(f"psum_free{i}") for i in range(4)]
        act_chain = sem("act_chain")
        dve_chain = sem("dve_chain")
        setup_done = sem("setup_done")
        setup_exp = sem("setup_exp")
        sp_ready = sem("sp_ready")
        half_mm = sem("half_mm")
        sq_ready = sem("sq_ready")
        sum_ready = sem("sum_ready")
        stat_post = sem("stat_post")
        rs_post = sem("rs_post")
        step_ready = sem("step_ready")
        h_ready = sem("h_ready")
        xh_ready = sem("xh_ready")
        xl_ready = sem("xl_ready")
        hsq_ready = sem("hsq_ready")
        hsum_ready = sem("hsum_ready")
        stat_pre = sem("stat_pre")
        rs_pre = sem("rs_pre")
        silu_ready = sem("silu_ready")
        hid_ready = sem("hid_ready")
        hidh_ready = sem("hidh_ready")
        hidl_ready = sem("hidl_ready")
        xc_ready = sem("xc_ready")
        xch_ready = sem("xch_ready")
        xcl_ready = sem("xcl_ready")
        qsum_ready = sem("qsum_ready")
        kvsum_ready = sem("kvsum_ready")
        cqh_ready = sem("cqh_ready")
        cql_ready = sem("cql_ready")
        stat_mix = sem("stat_mix")
        rs_q = sem("rs_q")
        rs_kv = sem("rs_kv")
        ckvn_ready = sem("ckvn_ready")
        ckvh_ready = sem("ckvh_ready")
        ckvl_ready = sem("ckvl_ready")
        gate_mm = sem("gate_mm")
        decay_ready = sem("decay_ready")
        lru_c = sem("lru_c")
        lru_root = sem("lru_root")
        gelu_ready = sem("gelu_ready")
        y_ready = sem("y_ready")
        ysq_ready = sem("ysq_ready")
        lsum_ready = sem("lsum_ready")
        rs_lru = sem("rs_lru")
        yn_ready = sem("yn_ready")
        ylh_ready = sem("ylh_ready")
        yll_ready = sem("yll_ready")
        sel_mm = sem("sel_mm")
        krope_ready = sem("krope_ready")
        v_mm = sem("v_mm")
        k_mm = sem("k_mm")
        q_mm = sem("q_mm")
        s0_mm = sem("s0_mm")
        s0_max = sem("s0_max")
        s0_exp = sem("s0_exp")
        t0_mm = sem("t0_mm")
        t0_copied = sem("t0_copied")
        o0_mm = sem("o0_mm")
        s_mm = sem("s_mm")
        max_ready = sem("max_ready")
        prob_ready = sem("prob_ready")
        t_mm = sem("t_mm")
        t_act = sem("t_act")
        t_dve = sem("t_dve")
        pv_mm = sem("pv_mm")
        o_copied = sem("o_copied")
        osq_ready = sem("osq_ready")
        osum_ready = sem("osum_ready")
        rs_att0 = sem("rs_att0")
        rs_att = sem("rs_att")
        on_ready = sem("on_ready")
        tr_mm = sem("tr_mm")
        yah_ready = sem("yah_ready")
        out_done = sem("out_done")

        class Chain:

            def __init__(self, eng, s):
                self.eng, self.s, self.n = eng, s, 0

            def link(self, ins):
                self.n += 1
                ins.then_inc(self.s, 1)
                self.eng.wait_ge(self.s, self.n)

        NQ = 4
        ITEMS = HEADS * NQ
        EARLY = HEADS - 2
        OSQ = 2 * NQ

        def keys_of(i):
            return N_META + i * P

        def copied_by_act(i):
            return i <= 2

        def place(e):
            hd, i = e // NQ, e % NQ
            return 2 * 1024 if i == NQ - 1 else (3 * hd + i) % 4 * 512

        def before(e):
            hd, i = e // NQ, e % NQ
            if i == NQ - 1:
                return e - NQ if hd else None
            n = 3 * hd + i - 4
            return n // 3 * NQ + n % 3 if n >= 0 else None

        def score_cols(e):
            c0, nk = place(e), keys_of(e % NQ + 1)
            if e % NQ < NQ - 1:
                return ps[:, c0:c0 + nk]
            return ps[:, c0:c0 + 1024].rearrange("p (a b) -> p a b", a=2)[:, :, 0:HALF]

        def turned_cols(e):
            return ps[:, place(e):place(e) + (e % NQ + 2) * P]

        def meta_turned(c, n):
            return ps[0:N_META, 3 * 512 + c:3 * 512 + c + n]

        def block_of(j):
            return (0, N_META) if j == 0 else (N_META + (j - 1) * P, P)

        def n_meta_layers(l):
            return l

        block = ctx.enter_context(nc.Block())

        @block.sync
        def _(sp):
            def load(n, src, adv=0):
                sp.wait_ge(slots_used, n + 1 + adv)
                k = tiles[n] * P
                sp.dma_start(raw[:, n % RING, 0:k], src).then_inc(raw_full[n % RING], 16)

            for b in range(NB):
                l, s0 = b // 3, slot0[b]
                if b % 3 == 1:
                    for n in range(S_OUT):
                        if n < S_GATE:
                            src = a["w_in"][l, n]
                        elif n == S_GATE:
                            src = a["w_gates"][l]
                        elif n < S_V:
                            src = a["w_in"][l, n - 1]
                        elif n == S_V:
                            src = a["w_v"][l]
                        elif n == S_K:
                            src = a["w_k"][l]
                        else:
                            src = a["w_q"][l, n - S_Q]
                        load(s0 + n, src)
                        if n == RING:
                            sp.dma_start(ropet[1][:, :], a["rope"][1]).then_inc(rope1_in, 16)
                        if n == S_V:
                            sp.wait_ge(cql_ready, QC * (l + 1))
                            sp.dma_start(ropet[0][:, :], a["rope"][0]).then_inc(rope0_in, 16)
                    with sp.Fori(0, DC // 4) as j:
                        for m in range(4):
                            load(s0 + S_OUT + m, a["w_out"][l, j * 4 + m], j * 4)
                else:
                    name = "ffn1" if b % 3 == 0 else "ffn2"
                    with sp.Fori(0, FC // 2) as j:
                        for m in range(2):
                            load(s0 + 2 * m, a[name + "_gate"][l, j * 2 + m], j * 4)
                            load(s0 + 2 * m + 1, a[name + "_up"][l, j * 2 + m], j * 4)
                    with sp.Fori(0, DC // 2) as j:
                        for m in range(2):
                            for q in range(2):
                                load(s0 + 2 * FC + 2 * m + q, a[name + "_down"][l, j * 2 + m, q], j * 4)
            for s in range(2):
                for k in range(DC):
                    sp.wait_ge(h_ready, seam_n(NB - 1, s, k))
                    sp.dma_start(out[k][:, s * (SEQ // 2):(s + 1) * (SEQ // 2)], half(h[:, k, :], True, s))\
                        .then_inc(out_done, 16)
            sp.wait_ge(out_done, 16 * 2 * DC)

        @block.gpsimd
        def _(pool):
            def lo(n, adv=0):
                pool.wait_ge(hi_ready, n + 1 + adv)
                r, k = n % RING, tiles[n] * P
                nc.gpsimd.tensor_tensor(wlo[:, r, 0:k], raw[:, r, 0:k], whi[:, r, 0:k].bitcast(F32),
                                        ALU.subtract).then_inc(lo_ready, 1)

            def lo_run(first, last):
                n = first
                while n < last:
                    k = n
                    while k < last and tiles[k] == tiles[n]:
                        k += 1
                    rounds = (k - n) // RING
                    if rounds > 1:
                        with pool.Fori(0, rounds) as j:
                            for m in range(RING):
                                lo(n + m, j * RING)
                        n += rounds * RING
                    while n < k:
                        lo(n)
                        n += 1

            def seam(b):
                trim = b > 0 and trimmed(b - 1)
                order = POOL_ORDER[split[b - 1] if b else 0]
                for s in range(2):
                    hs = half(tmp[4], trim, s)
                    for k in range(1, DC):
                        for q in order.get((s, k), ()):
                            lo(slot0[b] + q)
                        pool.wait_ge(hsq_ready, seam_n(b, s, k))
                        if k > 1:
                            pool.wait_ge(hsum_ready, hsum_n(b, s, k - 1))
                        nc.gpsimd.tensor_tensor(hs, hs, square_of(k, s, trim), ALU.add)\
                            .then_inc(hsum_ready, 1)
            for b in range(NB):
                seam(b)
                lo_run(slot0[b] + RING, slot0[b + 1] if b + 1 < NB else NSLOT)

        @block.scalar
        def _(act):
            chain = Chain(act, act_chain)
            act.dma_start(par[:, :, :], a["params"]).then_inc(par_in, 16)
            for i, (s, k0, nk) in enumerate(H_PARTS):
                act.dma_start(h[:, k0:k0 + nk, s * HALF:(s + 1) * HALF],
                              a["x"][k0:k0 + nk, :, s * HALF:(s + 1) * HALF].rearrange("k p t -> p k t"))\
                    .then_inc(h_in[i], 16)
                if i == 0:
                    act.dma_start(consts[:, :], a["consts"]).then_inc(consts_in, 16)

            def tables(i):
                act.add_instruction(mybir.InstLoadActFuncSet(name=nc.get_next_instruction_name(),
                                                             act_func_set_id=i, ins=[], outs=[]))

            def hi(n, adv=0):
                if n < NSLOT:
                    r, k = n % RING, tiles[n] * P
                    act.wait_ge(raw_full[r], 16 * (n // RING + 1) + adv * 4)
                    nc.scalar.activation(whi[:, r, 0:k], raw[:, r, 0:k], ACT.Copy).then_inc(hi_ready, 1)

            def inv_rms(dst, u, n, trim=False, bias=0.0):
                nc.scalar.activation(halves(dst, trim), unit(u, trim), ACT.Ln, scale=1.0 / n,
                                     bias=eps).then_inc(psum_free[pair_of(u)], 1)
                act.wait_ge(psum_free[pair_of(u)], read_out(u))
                return nc.scalar.activation(toks(dst, trim), toks(dst, trim), ACT.Exp, scale=-0.5, bias=bias)

            def inv_rms_half(dst, u, n, trim, s):
                ln = nc.scalar.activation(half(dst, trim, s), bank(u, trim, s), ACT.Ln, scale=1.0 / n,
                                          bias=eps)
                if s == 0:
                    chain.link(ln)
                else:
                    ln.then_inc(psum_free[pair_of(u)], 1)
                    act.wait_ge(psum_free[pair_of(u)], read_out(u))
                return nc.scalar.activation(half(dst, trim, s), half(dst, trim, s), ACT.Exp, scale=-0.5)

            def operand_half(b, k, s):
                l, trim = b // 3, b > 0 and trimmed(b - 1)
                g = ("ffn1_pre_g", "mix_pre_g", "ffn2_pre_g")[b % 3]
                if b == 0:
                    for i, (hs, k0, _) in enumerate(H_PARTS):
                        if (s, k) == (hs, k0):
                            act.wait_ge(h_in[i], 16)
                else:
                    act.wait_ge(h_ready, seam_n(b - 1, s, k))
                nc.scalar.activation(half(xh[:, k, :], trim, s), half(h[:, k, :], trim, s), ACT.Copy,
                                     scale=col(g, l, k)).then_inc(xh_ready, 1)
                ring = SQUARES[s]
                if k > ring:
                    act.wait_ge(hsum_ready, hsum_n(b, s, k - ring))
                nc.scalar.activation(square_of(k, s, trim), half(h[:, k, :], trim, s),
                                     ACT.Square).then_inc(hsq_ready, 1)

            def rs_pre_half(b, s):
                act.wait_ge(stat_pre, 2 * b + s + 1)
                inv_rms_half(rs_in, U[b, "pre"], D, b > 0 and trimmed(b - 1), s).then_inc(rs_pre, 1)

            def post_gain(b, m):
                return col("mix_post_g", b // 3, m) if b % 3 == 1 else half_g[:, b // 3, b % 3 // 2, m:m + 1]

            def output_chunk(b, m):
                trim, u = trimmed(b), U[b, "out"] + m
                act.wait_ge(slots_used, slot_used(out_slot(b, m)))
                if m >= 3:
                    act.wait_ge(sum_ready, sum_n(b, m - 2))
                sq = tmp[4] if m == 0 else tmp[m % 2]
                nc.scalar.activation(halves(sq, trim), unit(u, trim), ACT.Square).then_inc(sq_ready, 1)
                nc.scalar.activation(halves(f(b, m), trim), unit(u, trim), ACT.Copy,
                                     scale=post_gain(b, m)).then_inc(psum_free[pair_of(u)], 1)

            def output_half(b, m, s):
                l, trim, u = b // 3, trimmed(b), U[b, "out"] + m
                if s == 0:
                    act.wait_ge(half_mm, half_n(b, m))
                else:
                    act.wait_ge(slots_used, slot_used(out_slot(b, m)))
                act.wait_ge(sum_ready, sum_n(b, m - 2, s))
                nc.scalar.activation(half(tmp[m % 2], trim, s), bank(u, trim, s), ACT.Square)\
                    .then_inc(sq_ready, 1)
                ins = nc.scalar.activation(half(f(b, m), trim, s), bank(u, trim, s), ACT.Copy,
                                           scale=post_gain(b, m))
                if s == 1:
                    ins.then_inc(psum_free[pair_of(u)], 1)

            def rs_post_half(b, s):
                act.wait_ge(stat_post, 2 * (b - 1) + s + 1)
                inv_rms_half(tmp[2], U[b, "post"], D, trimmed(b - 1), s).then_inc(rs_post, 1)

            def seam(b):
                first = DC - split[b - 1] if b else DC
                order = ACT_ORDER[0 if b == 0 else split[b - 1]]
                def at(s, k):
                    for what, i in order.get((s, k), ()):
                        if what == "out":
                            output_half(b - 1, i, 1)
                        elif b < NB and what == "hi":
                            hi(slot0[b] + i)
                        elif b < NB:
                            rs_pre_half(b, 0)

                for m in range(first, DC):
                    output_half(b - 1, m, 0)
                    at(-1, m)
                for s in range(2):
                    if b > 0:
                        rs_post_half(b, s)
                    for k in range(DC):
                        at(s, k)
                        if b < NB:
                            operand_half(b, k, s)
                    at(s, DC)
                if b < NB:
                    rs_pre_half(b, 1)
                    tables(EXP_TANH_TABLES if b % 3 == 1 else SILU_TABLES)

            tables(LN_EXP_TABLES)
            act.wait_ge(setup_done, 1)
            nc.scalar.activation(small[:, 0:depth * WC], small[:, 0:depth * WC], ACT.Exp,
                                 scale=-1.0).then_inc(setup_exp, 1)

            def ffn(b):
                s0, f0 = slot0[b], (b // 3 * 2 + b % 3 // 2) * FC
                u0, trim = U[b, "gu"], b > 0 and trimmed(b - 1)

                def hidden(m, it=0):
                    adv = it * RING
                    ug = u0 + 2 * m
                    mm = m + 2 * it
                    act.wait_ge(psum_free[pair_of(ug)], read_out(ug) + it)
                    nc.scalar.activation(toks(tmp[2], trim), toks(tmp[0], trim), ACT.Silu).then_inc(silu_ready, 1)
                    hi(s0 + 2 * m + RING, adv)
                    act.wait_ge(hid_ready, f0 + mm + 1)
                    nc.scalar.activation(toks(hidh[:, mm, :], trim), toks(tmp[3], trim),
                                         ACT.Copy).then_inc(hidh_ready, 1)
                    hi(s0 + 2 * m + 1 + RING, adv)

                hidden(0)
                hidden(1)
                with act.Fori(0, FC // 2 - 2) as j:
                    hidden(2, j)
                    hidden(3, j)
                hidden(FC - 2)
                hidden(FC - 1)
                tables(LN_EXP_TABLES)
                for m in range(DC - split[b]):
                    hi(out_slot(b, m) - 1 + RING)
                    output_chunk(b, m)
                    hi(out_slot(b, m) + RING)

            def mixer(b):
                l, s0 = b // 3, slot0[b]
                hi(s0 + 4)
                hi(s0 + 5)
                for c in range(WC):
                    act.wait_ge(xc_ready, WC * l + c + 1)
                    nc.scalar.activation(xch[:, c, :], xc[:, c, :], ACT.Copy).then_inc(xch_ready, 1)
                    if c < 3:
                        hi(s0 + 6 + c)
                hi(s0 + 9)
                for g, dst in enumerate((rg, ig)):
                    for c in range(WC):
                        u = U[b, "gate"] + WC * g + c
                        if WC * g + c < 2 * WC - 1:
                            act.wait_ge(gate_mm, (2 * WC - 1) * l + WC * g + c + 1)
                        else:
                            act.wait_ge(slots_used, slot_used(s0 + S_GATE))
                        nc.scalar.activation(halves(dst[:, c, :], False), unit(u, False), ACT.Tanh,
                                             scale=0.5, bias=half_b[:, l, g, c:c + 1])\
                            .then_inc(psum_free[pair_of(u)], 1)
                    hi(s0 + 10 + g)
                for c in range(QC):
                    u = U[b, "cq"] + c
                    act.wait_ge(psum_free[pair_of(u)], read_out(u))
                    nc.scalar.activation(cqh[:, c, :], cq[:, c, :], ACT.Copy,
                                         scale=col("mla_q_norm_g", l, c)).then_inc(cqh_ready, 1)
                for c in range(WC):
                    u = U[b, "gate"] + c
                    A, nA = decay[:, 0, l, c:c + 1], decay[:, 1, l, c:c + 1]
                    act.wait_ge(psum_free[pair_of(u)], read_out(u))
                    nc.scalar.activation(av[:, c, :], rg[:, c, :], ACT.Exp, scale=A, bias=A)\
                        .then_inc(decay_ready, 1)
                    nc.scalar.activation(rg[:, c, :], rg[:, c, :], ACT.Tanh, scale=nA, bias=nA)\
                        .then_inc(decay_ready, 1)
                hi(s0 + 12)
                hi(s0 + 13)
                tables(LN_EXP_TABLES)
                act.wait_ge(stat_mix, 3 * l + 1)
                inv_rms(tmp[2], U[b, "statq"], QL, bias=ln_scale).then_inc(rs_q, 1)
                hi(s0 + 14)
                act.wait_ge(stat_mix, 3 * l + 2)
                inv_rms(tmp[3], U[b, "statkv"], KVL).then_inc(rs_kv, 1)
                for c in range(KVC):
                    act.wait_ge(ckvn_ready, KVC * l + c + 1)
                    nc.scalar.activation(ckvh[:, c, :], ckv[:, c, :], ACT.Copy,
                                         scale=col("mla_kv_norm_g", l, c)).then_inc(ckvh_ready, 1)
                hi(s0 + 15)
                for c in range(WC):
                    act.wait_ge(lru_c, WC * l + c + 1)
                    nc.scalar.activation(rg[:, c, :], rg[:, c, :], ACT.Sqrt, scale=0.25)\
                        .then_inc(lru_root, 1)
                for n in (16, 17, 18):
                    hi(s0 + n)
                for c in range(WC):
                    u = U[b, "gr"] + c
                    act.wait_ge(psum_free[pair_of(u)], read_out(u))
                    nc.scalar.activation(gr[:, c, :], gr[:, c, :], ACT.Gelu_apprx_tanh)\
                        .then_inc(gelu_ready, 1)
                act.wait_ge(sel_mm, l + 1)
                u = U[b, "sel"]
                nc.scalar.activation(halves(tmp[0], False), unit(u, False), ACT.Copy)\
                    .then_inc(psum_free[pair_of(u)], 1)
                for i in range(3):
                    u = U[b, "v"] + i
                    if i < 2:
                        act.wait_ge(v_mm, 2 * l + i + 1)
                    else:
                        act.wait_ge(slots_used, slot_used(s0 + S_V))
                    n = 2 if i < 2 else 1
                    nc.scalar.activation(vt[:, 2 * i:2 * i + n, :],
                                         pair(pair_of(u)).rearrange("p (a b) -> p a b", a=2)[:, 0:n, :],
                                         ACT.Copy).then_inc(psum_free[pair_of(u)], 1)
                hi(s0 + 19)
                for i in range(HEADS // 2):
                    u = U[b, "k"] + i
                    if i < HEADS // 2 - 1:
                        act.wait_ge(k_mm, (HEADS // 2 - 1) * l + i + 1)
                    else:
                        act.wait_ge(slots_used, slot_used(s0 + S_K))
                    nc.scalar.activation(halves(kt(2 * i)[0:NOPE], False), unit(u, False)[0:NOPE],
                                         ACT.Copy)
                    nc.scalar.activation(halves(kt(2 * i + 1)[NOPE:P], False), unit(u, False)[NOPE:P],
                                         ACT.Copy).then_inc(psum_free[pair_of(u)], 1)
                for c in range(WC):
                    act.wait_ge(y_ready, WC * l + c + 1)
                    nc.scalar.activation(ig[:, c, :], xc[:, c, :], ACT.Square).then_inc(ysq_ready, 1)
                tables(LN_EXP_TABLES)
                hi(s0 + 20)
                act.wait_ge(stat_mix, 3 * l + 3)
                inv_rms(tmp[4], U[b, "statl"], W).then_inc(rs_lru, 1)
                for c in range(WC):
                    act.wait_ge(yn_ready, WC * l + c + 1)
                    nc.scalar.activation(ylh[:, c, :], xc[:, c, :], ACT.Copy,
                                         scale=col("lru_out_g", l, c)).then_inc(ylh_ready, 1)
                for n in (21, 22, 23):
                    hi(s0 + n)

                if not trimmed(b):
                    m0 = n_meta_layers(l)
                    act.wait_ge(s0_max, 2 * m0 + 2)
                    nc.scalar.activation(prob[3][0:N_META, 0:P], prob[3][0:N_META, 0:P], ACT.Exp)\
                        .then_inc(s0_exp, 1)
                n_sq = OSQ * l + n_meta_layers(l)
                for e in range(ITEMS + 2):
                    if e >= 2 and copied_by_act((e - 2) % NQ + 1):
                        transposed_copy_act(l, e - 2)
                    if e < ITEMS:
                        E, i = ITEMS * l + e, e % NQ + 1
                        dst = prob[e % 4][:, 0:keys_of(i)] if i < NQ else halves(prob[e % 4], False)
                        act.wait_ge(max_ready, E + 1)
                        if e >= 4:
                            act.wait_ge(t_mm, E - 3)
                        elif e == 3 and not trimmed(b):
                            act.wait_ge(t0_mm, n_meta_layers(l) + 1)
                        nc.scalar.activation(dst, score_cols(e), ACT.Exp, bias=small[:, 8 + e % 4:9 + e % 4],
                                             accum_out=small[:, 16 + e % 8:17 + e % 8])\
                            .then_inc(prob_ready, 1)
                    if e == 3:
                        hi(s0 + 24)
                    i = e - (ITEMS - NQ)
                    if 0 <= i < NQ:
                        act.wait_ge(o_copied, HEADS * l + EARLY)
                        nc.scalar.activation(tmp[i][:, 0:EARLY * VD], osb[:, i, 0:EARLY * VD], ACT.Square,
                                             accum_out=small[:, 24 + i:25 + i]).then_inc(osq_ready, 1)
                        n_sq += 1
                    if i == 0 and not trimmed(b):
                        act.wait_ge(t0_copied, 2 * (n_meta_layers(l) + 1))
                        nc.scalar.activation(rs_in[0:N_META, 0:W], osb0[0:N_META, :], ACT.Square,
                                             accum_out=small[0:N_META, 28:29]).then_inc(osq_ready, 1)
                        n_sq += 1
                        act.wait_ge(osq_ready, n_sq)
                        chain.link(nc.scalar.activation(small[0:N_META, 36:37], small[0:N_META, 28:29],
                                                        ACT.Ln, scale=1.0 / W, bias=eps[0:N_META]))
                        nc.scalar.activation(small[0:N_META, 36:37], small[0:N_META, 36:37],
                                             ACT.Exp, scale=-0.5).then_inc(rs_att0, 1)
                act.wait_ge(o_copied, HEADS * (l + 1))
                for i in range(NQ):
                    nc.scalar.activation(tmp[i][:, EARLY * VD:W], osb[:, i, EARLY * VD:W], ACT.Square,
                                         accum_out=small[:, 60 + i:61 + i]).then_inc(osq_ready, 1)
                act.wait_ge(osum_ready, l + 1)
                chain.link(nc.scalar.activation(small[:, 32:36], small[:, 24:28], ACT.Ln,
                                                scale=1.0 / W, bias=eps))
                nc.scalar.activation(small[:, 32:36], small[:, 32:36], ACT.Exp, scale=-0.5)\
                    .then_inc(rs_att, 1)
                for c in range(WC):
                    act.wait_ge(tr_mm, WC * l + c + 1)
                    pr, g = pair(pair_of(U[b, "tr"] + c)), col("mla_out_g", l, c)
                    if not trimmed(b):
                        nc.scalar.activation(xh[:, WC + c, 0:N_META], pr[:, 512:512 + N_META], ACT.Copy,
                                             scale=g)
                    nc.scalar.activation(xh[:, WC + c, N_META:T], pr[:, 0:SEQ], ACT.Copy, scale=g)\
                        .then_inc(yah_ready, 1)
                for m in range(DC - split[b]):
                    output_chunk(b, m)
                    if m < RING:
                        hi(out_slot(b, m) + RING)

            def transposed_copy_act(l, e):
                E, i = ITEMS * l + e, e % NQ + 1
                act.wait_ge(t_mm, E + 1)
                if e >= 3:
                    act.wait_ge(pv_mm, E - 2)
                nc.scalar.activation(probT[e % 3][:, 0:(i + 1) * P], turned_cols(e), ACT.Copy).then_inc(t_act, 1)

            for b in range(NB):
                seam(b)
                if b % 3 == 1:
                    mixer(b)
                else:
                    ffn(b)
            seam(NB)

        @block.vector
        def _(dve):
            chain = Chain(dve, dve_chain)
            nc.vector.memset(maskb[:, :], 0.0).then_inc(zeros_ready, 1)
            dve.wait_ge(par_in, 16)
            lam = par[:, :, PCOL["lru_lambda"]:PCOL["lru_lambda"] + WC]

            def sm(i):
                return small[:, i * depth * WC:(i + 1) * depth * WC].rearrange("p (l c) -> p l c", l=depth)

            chain.link(nc.vector.tensor_scalar(sm(1), lam, -1.0, None, ALU.mult))
            nc.vector.tensor_tensor(sm(0), lam, sm(1), ALU.max).then_inc(setup_done, 1)
            for i, name in enumerate(("ffn1_post_g", "ffn2_post_g")):
                nc.vector.tensor_scalar(half_g[:, :, i, :], par[:, :, PCOL[name]:PCOL[name] + DC],
                                        0.5, None, ALU.mult)
            for i, name in enumerate(("lru_b_a", "lru_b_x")):
                nc.vector.tensor_scalar(half_b[:, :, i, :], par[:, :, PCOL[name]:PCOL[name] + WC],
                                        0.5, None, ALU.mult)
            def decay_rates():
                chain.link(nc.vector.tensor_scalar(sm(1), sm(1), 0.0, None, ALU.max))
                dve.wait_ge(setup_exp, 1)
                chain.link(nc.vector.tensor_scalar(sm(2), sm(0), 2.0, None, ALU.add))
                chain.link(nc.vector.reciprocal(sm(2), sm(2)))
                chain.link(nc.vector.tensor_tensor(sm(2), sm(0), sm(2), ALU.mult))
                chain.link(nc.vector.tensor_tensor(sm(3), sm(2), sm(2), ALU.mult))
                terms = [1.0 / (2 * i + 1) for i in range(9)]
                chain.link(nc.vector.tensor_scalar(sm(0), sm(3), terms[8], terms[7], ALU.mult, ALU.add))
                for i in range(6, -1, -1):
                    chain.link(nc.vector.tensor_tensor(sm(0), sm(0), sm(3), ALU.mult))
                    chain.link(nc.vector.tensor_scalar(sm(0), sm(0), terms[i], None, ALU.add))
                chain.link(nc.vector.tensor_tensor(sm(0), sm(0), sm(2), ALU.mult))
                chain.link(nc.vector.scalar_tensor_tensor(sm(0), sm(0), 2.0, sm(1), ALU.mult, ALU.add))
                nc.vector.tensor_scalar(decay[:, 0, :, :], sm(0), -LRU_C / 2, None, ALU.mult)
                nc.vector.tensor_scalar(decay[:, 1, :, :], sm(0), LRU_C / 2, None, ALU.mult)\
                    .then_inc(sp_ready, 1)
                dve.wait_ge(consts_in, 16)
                nc.vector.tensor_copy(identb[:, :], ident)
                nc.vector.tensor_copy(maskb[:, :], consts[:, C_MASK:C_MASK + P])

            def seam(b):
                l, trim = b // 3, b > 0 and trimmed(b - 1)
                g = ("ffn1_pre_g", "mix_pre_g", "ffn2_pre_g")[b % 3]

                def scratch(k, s):
                    return tmp[3][:, k % 2 * HALF:k % 2 * HALF + span(trim, s)[1]]

                def step(k, s):
                    if k >= 2 or s == 1:
                        dve.wait_ge(h_ready, seam_n(b - 1, s, k - 2))
                    nc.vector.tensor_tensor(scratch(k, s), half(f(b - 1, k), trim, s),
                                            half(tmp[2], trim, s), ALU.mult).then_inc(step_ready, 1)

                def residual(k, s):
                    dve.wait_ge(step_ready, seam_n(b - 1, s, k))
                    hk = half(h[:, k, :], trim, s)
                    nc.vector.tensor_tensor(hk, hk, scratch(k, s), ALU.add).then_inc(h_ready, 1)

                def operand_lo(k, s):
                    dve.wait_ge(xh_ready, seam_n(b, s, k))
                    nc.vector.scalar_tensor_tensor(half(xl[:, k, :], trim, s), half(h[:, k, :], trim, s),
                                                   col(g, l, k), half(xh[:, k, :], trim, s).bitcast(F32),
                                                   ALU.mult, ALU.subtract).then_inc(xl_ready, 1)

                for s in range(2):
                    if b > 0:
                        dve.wait_ge(rs_post, 2 * (b - 1) + s + 1)
                        step(0, s)
                    for k in range(DC + 1):
                        if b > 0 and k + 1 < DC:
                            step(k + 1, s)
                        if b > 0 and k < DC:
                            residual(k, s)
                        if k and b < NB:
                            operand_lo(k - 1, s)
                        if b > 0 and s == 0 and k == DC // 2:
                            add_square(b - 1, DC - split[b - 1], 1)
                        if b > 0 and s == 0 and k == DC and split[b - 1] == 3:
                            add_square(b - 1, DC - 2, 1)

            def add_square(b, m, s=None):
                trim = trimmed(b)
                part = toks if s is None else lambda t2, trim: half(t2, trim, s)
                n = 1 if s is None else s
                dve.wait_ge(sq_ready, sq_n(b, m, n))
                if m >= 2:
                    dve.wait_ge(sum_ready, sum_n(b, m - 1, n))
                acc = part(tmp[4], trim)
                nc.vector.tensor_tensor(acc, acc, part(tmp[m % 2], trim), ALU.add).then_inc(sum_ready, 1)

            def output_sum(b):
                for m in range(1, DC - split[b]):
                    add_square(b, m)
                for m in range(DC - split[b], DC - 1):
                    add_square(b, m, 0)

            def ffn(b):
                s0, f0 = slot0[b], (b // 3 * 2 + b % 3 // 2) * FC
                u0, trim = U[b, "gu"], b > 0 and trimmed(b - 1)

                def hidden(m, it=0):
                    adv, mm = it * RING, m + 2 * it
                    ug, uu = u0 + 2 * m, u0 + 2 * m + 1
                    dve.wait_ge(slots_used, slot_used(s0 + 2 * m) + adv)
                    nc.vector.tensor_tensor(halves(tmp[0], trim), unit(ug, trim), halves(rs_in, trim),
                                            ALU.mult).then_inc(psum_free[pair_of(ug)], 1)
                    dve.wait_ge(slots_used, slot_used(s0 + 2 * m + 1) + adv)
                    nc.vector.tensor_tensor(halves(tmp[1], trim), unit(uu, trim), halves(rs_in, trim),
                                            ALU.mult).then_inc(psum_free[pair_of(uu)], 1)
                    dve.wait_ge(psum_free[pair_of(uu)], read_out(uu) + it)
                    dve.wait_ge(silu_ready, f0 + mm + 1)
                    nc.vector.tensor_tensor(toks(tmp[3], trim), toks(tmp[2], trim), toks(tmp[1], trim),
                                            ALU.mult).then_inc(hid_ready, 1)
                    dve.wait_ge(hidh_ready, f0 + mm + 1)
                    nc.vector.tensor_tensor(toks(hidl[:, mm, :], trim), toks(tmp[3], trim),
                                            toks(hidh[:, mm, :], trim).bitcast(F32),
                                            ALU.subtract).then_inc(hidl_ready, 1)

                dve.wait_ge(rs_pre, 2 * (b + 1))
                hidden(0)
                if b == 0:
                    decay_rates()
                hidden(1)
                with dve.Fori(0, FC // 2 - 1) as j:
                    hidden(2, j)
                    hidden(3, j)
                output_sum(b)

            def scaled(dst, u, n):
                dve.wait_ge(slots_used, slot_used(n))
                nc.vector.tensor_tensor(halves(dst, False), unit(u, False), halves(rs_in, False),
                                        ALU.mult).then_inc(psum_free[pair_of(u)], 1)
                dve.wait_ge(psum_free[pair_of(u)], read_out(u))

            def mixer(b):
                l, s0 = b // 3, slot0[b]
                dve.wait_ge(rs_pre, 2 * (b + 1))
                dve.wait_ge(slots_used, slot_used(s0))
                nc.vector.memset(xr[:, :, 0:CONV - 1], 0.0)
                for c in range(WC):
                    scaled(xr[:, c, CONV - 1:], U[b, "xr"] + c, s0 + S_XR + c)
                    x = xc[:, c, :]
                    cw = "lru_conv_w"
                    chain.link(nc.vector.tensor_scalar(x, xr[:, c, CONV - 1:], col(cw, l, (CONV - 1) * WC + c),
                                                       col("lru_conv_b", l, c), ALU.mult, ALU.add))
                    for k in range(CONV - 1):
                        ins = nc.vector.scalar_tensor_tensor(x, xr[:, c, k:k + T], col(cw, l, k * WC + c), x,
                                                             ALU.mult, ALU.add)
                        if k < CONV - 2:
                            chain.link(ins)
                        else:
                            ins.then_inc(xc_ready, 1)
                for c in range(WC):
                    dve.wait_ge(xch_ready, WC * l + c + 1)
                    nc.vector.tensor_tensor(xcl[:, c, :], xc[:, c, :], xch[:, c, :].bitcast(F32),
                                            ALU.subtract).then_inc(xcl_ready, 1)
                square_sum(b, "cq", cq, QC, s0 + S_CQ, tmp[0], qsum_ready)
                square_sum(b, "ckv", ckv, KVC, s0 + S_CKV, tmp[1], kvsum_ready)
                for c in range(QC):
                    dve.wait_ge(cqh_ready, QC * l + c + 1)
                    nc.vector.scalar_tensor_tensor(cql[:, c, :], cq[:, c, :], col("mla_q_norm_g", l, c),
                                                   cqh[:, c, :].bitcast(F32), ALU.mult,
                                                   ALU.subtract).then_inc(cql_ready, 1)
                dve.wait_ge(decay_ready, 2 * WC * (l + 1))
                for c in range(WC):
                    chain.link(nc.vector.scalar_tensor_tensor(ig[:, c, :], ig[:, c, :], 1.0, xc[:, c, :],
                                                              ALU.add, ALU.mult))
                    chain.link(nc.vector.tensor_tensor(xc[:, c, :], av[:, c, :], av[:, c, :], ALU.mult))
                    nc.vector.scalar_tensor_tensor(rg[:, c, :], xc[:, c, :], 1.0, rg[:, c, :],
                                                   ALU.add, ALU.mult).then_inc(lru_c, 1)
                dve.wait_ge(rope1_in, 16 * (l + 1))
                kr2 = 2 * ROPE
                chain.link(nc.vector.tensor_tensor(tmp[4][0:kr2], ropet[1][0:kr2], rs_in[0:kr2], ALU.mult))
                u = U[b, "kr"]
                dve.wait_ge(slots_used, slot_used(s0 + S_KR))
                nc.vector.tensor_tensor(halves(tmp[4][0:kr2], False), unit(u, False)[0:kr2],
                                        halves(tmp[4][0:kr2], False), ALU.mult)\
                    .then_inc(psum_free[pair_of(u)], 1)
                scaled(gr[:, 0, :], U[b, "gr"], s0 + S_GR)
                dve.wait_ge(rs_kv, l + 1)
                for c in range(KVC):
                    nc.vector.tensor_tensor(ckv[:, c, :], ckv[:, c, :], tmp[3][:, :], ALU.mult)\
                        .then_inc(ckvn_ready, 1)
                for c in range(KVC):
                    dve.wait_ge(ckvh_ready, KVC * l + c + 1)
                    nc.vector.scalar_tensor_tensor(ckvl[:, c, :], ckv[:, c, :], col("mla_kv_norm_g", l, c),
                                                   ckvh[:, c, :].bitcast(F32), ALU.mult,
                                                   ALU.subtract).then_inc(ckvl_ready, 1)
                for c in range(WC):
                    if c:
                        scaled(gr[:, c, :], U[b, "gr"] + c, s0 + S_GR + c)
                    dve.wait_ge(lru_root, WC * l + c + 1)
                    chain.link(nc.vector.tensor_tensor(rg[:, c, :], rg[:, c, :], ig[:, c, :], ALU.mult))
                    nc.vector.tensor_tensor_scan(xc[:, c, :], av[:, c, :], rg[:, c, :], 0.0,
                                                 ALU.mult, ALU.add)
                dve.wait_ge(rs_q, l + 1)
                dve.wait_ge(rope0_in, 16 * (l + 1))
                for i in range(2):
                    chain.link(nc.vector.tensor_tensor(ropet[i][:, :], ropet[i][:, :], tmp[2][:, :],
                                                       ALU.mult))
                for c in range(WC):
                    dve.wait_ge(gelu_ready, WC * l + c + 1)
                    nc.vector.tensor_tensor(xc[:, c, :], xc[:, c, :], gr[:, c, :], ALU.mult)\
                        .then_inc(y_ready, 1)
                u = U[b, "sel"]
                dve.wait_ge(psum_free[pair_of(u)], read_out(u))
                for i, (p0, p1) in enumerate(((NOPE, P), (0, NOPE))):
                    nc.vector.tensor_copy(kt_of[i][p0:p1, :, :],
                                          tmp[0][p0:p1, :].unsqueeze(1).broadcast_to([NOPE, 4, T]))\
                        .then_inc(krope_ready, 1)
                for c in range(1, WC):
                    dve.wait_ge(ysq_ready, WC * l + c + 1)
                    if c > 1:
                        dve.wait_ge(lsum_ready, 3 * l + c - 1)
                    nc.vector.tensor_tensor(ig[:, 0, :], ig[:, 0, :], ig[:, c, :], ALU.add)\
                        .then_inc(lsum_ready, 1)

                def queries(hd):
                    u = unit_q(b, hd)
                    if hd % 2 == 0:
                        dve.wait_ge(q_mm, HEADS // 2 * l + hd // 2 + 1)
                    else:
                        dve.wait_ge(slots_used, slot_used(s0 + S_Q + hd // 2))
                    nc.vector.tensor_tensor(halves(qt(hd), False), unit(u, False),
                                            halves(ropet[hd % 2], False), ALU.mult)\
                        .then_inc(psum_free[pair_of(u)], 1)

                for hd in range(HEADS // 2):
                    queries(hd)
                dve.wait_ge(rs_lru, l + 1)
                for c in range(WC):
                    nc.vector.tensor_tensor(xc[:, c, :], xc[:, c, :], tmp[4][:, :], ALU.mult)\
                        .then_inc(yn_ready, 1)
                queries(4)
                queries(5)

                def lru_lo(c):
                    dve.wait_ge(ylh_ready, WC * l + c + 1)
                    nc.vector.scalar_tensor_tensor(yll[:, c, :], xc[:, c, :], col("lru_out_g", l, c),
                                                   ylh[:, c, :].bitcast(F32), ALU.mult,
                                                   ALU.subtract).then_inc(yll_ready, 1)

                for c in range(WC - 1):
                    lru_lo(c)
                queries(6)
                queries(7)

                m0, nm = n_meta_layers(l), N_META
                mx, dn = small[0:nm, 40:48], small[0:nm, 48:56]
                p0 = prob[3][0:nm, 0:P].rearrange("p (h k) -> p h k", h=HEADS)

                def meta_maxima():
                    s0p = meta_turned(0, P).rearrange("p (h k) -> p h k", h=HEADS)
                    dve.wait_ge(s0_mm, m0 + 1)
                    nc.vector.tensor_reduce(mx, s0p, AX.X, ALU.max).then_inc(s0_max, 1)
                    dve.wait_ge(s0_max, 2 * m0 + 1)
                    nc.vector.tensor_tensor(p0, s0p, mx.unsqueeze(2).broadcast_to([nm, HEADS, nm]),
                                            ALU.subtract).then_inc(s0_max, 1)

                def meta_copy():
                    dve.wait_ge(s0_exp, m0 + 1)
                    chain.link(nc.vector.tensor_reduce(dn, p0, AX.X, ALU.add))
                    dve.wait_ge(t0_mm, m0 + 1)
                    nc.vector.tensor_copy(probT[2][0:nm, 0:P], meta_turned(0, P)).then_inc(t0_copied, 1)
                    chain.link(nc.vector.reciprocal(dn, dn))

                def meta_outputs():
                    dve.wait_ge(o0_mm, m0 + 1)
                    nc.vector.tensor_tensor(
                        osb0[0:nm, :].rearrange("p (h d) -> p h d", h=HEADS),
                        ps[0:nm, 7 * 512:8 * 512].rearrange("p (h d) -> p h d", h=HEADS),
                        dn.unsqueeze(2).broadcast_to([nm, HEADS, VD]), ALU.mult).then_inc(t0_copied, 1)

                def head_out(hd):
                    H = HEADS * l + hd
                    rd = small[:, 56:60]
                    dve.wait_ge(pv_mm, ITEMS * l + NQ * (hd + 1))
                    chain.link(nc.vector.reciprocal(rd, small[:, 16 + NQ * (hd % 2):20 + NQ * (hd % 2)]))
                    nc.vector.tensor_tensor(
                        osb[:, :, hd * VD:(hd + 1) * VD],
                        pair(3)[:, (hd % 2) * 512:(hd % 2) * 512 + NQ * VD].rearrange("p (i d) -> p i d", i=NQ),
                        rd.unsqueeze(2).broadcast_to([P, NQ, VD]), ALU.mult).then_inc(o_copied, 1)

                if not trimmed(b):
                    meta_maxima()
                for e in range(ITEMS + 3):
                    if e == 4 and not trimmed(b):
                        meta_outputs()
                    q = e - 2
                    if 0 <= q < ITEMS and not copied_by_act(q % NQ + 1):
                        Q, i = ITEMS * l + q, q % NQ + 1
                        dve.wait_ge(t_mm, Q + 1)
                        if q >= 3:
                            dve.wait_ge(pv_mm, Q - 2)
                        nc.vector.tensor_copy(probT[q % 3][:, 0:(i + 1) * P], turned_cols(q))\
                            .then_inc(t_dve, 1)
                    if e < ITEMS:
                        E, i = ITEMS * l + e, e % NQ + 1
                        dve.wait_ge(s_mm, E + 1)
                        if e >= 4:
                            dve.wait_ge(prob_ready, E - 3)
                        nc.vector.tensor_reduce(small[:, 8 + e % 4:9 + e % 4], score_cols(e),
                                                AX.X if i < NQ else AX.XY, ALU.max,
                                                negate=True).then_inc(max_ready, 1)
                    if e == 2 and not trimmed(b):
                        meta_copy()
                    if e == 5:
                        lru_lo(WC - 1)
                    if e >= 3 and (e - 3) % NQ == NQ - 1:
                        head_out((e - 3) // NQ)
                if not trimmed(b):
                    dve.wait_ge(rs_att0, n_meta_layers(l) + 1)
                    nc.vector.tensor_scalar(osb0[0:N_META, :], osb0[0:N_META, :], small[0:N_META, 36:37],
                                            None, ALU.mult).then_inc(on_ready, 1)
                dve.wait_ge(osq_ready, OSQ * (l + 1) + n_meta_layers(l) + (0 if trimmed(b) else 1))
                nc.vector.tensor_tensor(small[:, 24:28], small[:, 24:28], small[:, 60:64], ALU.add)\
                    .then_inc(osum_ready, 1)
                dve.wait_ge(rs_att, l + 1)
                for c in range(WC):
                    o = osb[:, :, c * P:(c + 1) * P]
                    nc.vector.tensor_tensor(o, o, small[:, 32:36].unsqueeze(2).broadcast_to([P, NQ, P]),
                                            ALU.mult).then_inc(on_ready, 1)
                for c in range(WC):
                    dve.wait_ge(yah_ready, WC * l + c + 1)
                    u = U[b, "tr"] + c
                    pr, g = pair(pair_of(u)), col("mla_out_g", l, c)
                    if not trimmed(b):
                        nc.vector.scalar_tensor_tensor(xl[:, WC + c, 0:N_META], pr[:, 512:512 + N_META], g,
                                                       xh[:, WC + c, 0:N_META].bitcast(F32), ALU.mult,
                                                       ALU.subtract)
                    nc.vector.scalar_tensor_tensor(xl[:, WC + c, N_META:T], pr[:, 0:SEQ], g,
                                                   xh[:, WC + c, N_META:T].bitcast(F32), ALU.mult,
                                                   ALU.subtract).then_inc(psum_free[pair_of(u)], 1)
                output_sum(b)

            def square_sum(b, name, z, nch, n0, acc, done):
                for c in range(nch):
                    scaled(z[:, c, :], U[b, name] + c, n0 + c)
                    if c == 0:
                        chain.link(nc.vector.tensor_tensor(acc[:, :], z[:, c, :], z[:, c, :], ALU.mult))
                    else:
                        chain.link(nc.vector.tensor_tensor(tmp[4][:, :], z[:, c, :], z[:, c, :], ALU.mult))
                        ins = nc.vector.tensor_tensor(acc[:, :], acc[:, :], tmp[4][:, :], ALU.add)
                        if c == nch - 1:
                            ins.then_inc(done, 1)
                        else:
                            chain.link(ins)

            for b in range(NB):
                seam(b)
                if b % 3 == 1:
                    mixer(b)
                else:
                    ffn(b)
            seam(NB)

        @block.tensor
        def _(pe):
            pe.sem_inc(slots_used, RING)
            for i in range(4):
                pe.sem_inc(psum_free[i], 1)
            pe.wait_ge(zeros_ready, 1)
            with pe.Fori(0, WARM_UP // 8):
                for _ in range(8):
                    nc.tensor.matmul(pair(3)[:, 0:P], maskb[:, :], maskb[:, :], start=True, stop=True)

            def mm(o, w, x, start, stop):
                return nc.tensor.matmul(o, w, x, start=start, stop=stop)

            def tile(u, n, t, xhk, xlk, grp, first, last):
                pr, r = pair(pair_of(u)), n % RING
                wh, wl = whi[:, r, t * P:(t + 1) * P], wlo[:, r, t * P:(t + 1) * P]
                for w, x, start, stop in ((wh, xhk, first, False), (wh, xlk, False, False),
                                          (wl, xhk, False, last)):
                    for t0, nt, c0 in grp:
                        ins = mm(pr[:, c0:c0 + nt], w, x[:, t0:t0 + nt], start, stop)
                return ins

            def slot_in(n, adv=0):
                pe.wait_ge(lo_ready, n + 1 + adv)

            def unit_free(u, it=0):
                pe.wait_ge(psum_free[pair_of(u)], free_for(u) + it)

            def product(u, n, trim, adv=0, it=0, led=False, leads=False):
                slot_in(n, adv)
                if not led:
                    unit_free(u, it)
                for k in range(DC):
                    if leads and k == DC - 1:
                        unit_free(u + 1, it)
                    ins = tile(u, n, k, xh[:, k, :], xl[:, k, :], groups(trim), k == 0, k == DC - 1)
                ins.then_inc(slots_used, 1)

            def opening(b, u, n, trim):
                first, second = groups(trim)
                for q in range(3):
                    slot_in(n + q)
                    unit_free(u + q)
                    for k in range(DC):
                        if q == 0:
                            pe.wait_ge(xl_ready, seam_n(b, 0, k))
                        tile(u + q, n + q, k, xh[:, k, :], xl[:, k, :], [first], k == 0, k == DC - 1)
                    if q == 0 and b > 0:
                        stat_out(b - 1, 1)
                stat_in(b, 0)
                for k in range(DC - 2):
                    pe.wait_ge(xl_ready, seam_n(b, 1, k))
                    for q in range(3):
                        tile(u + q, n + q, k, xh[:, k, :], xl[:, k, :], [second], k == 0, False)
                for q in range(3):
                    if q == 2:
                        stat_in(b, 1)
                    for k in range(DC - 2, DC):
                        if q == 0:
                            pe.wait_ge(xl_ready, seam_n(b, 1, k))
                        ins = tile(u + q, n + q, k, xh[:, k, :], xl[:, k, :], [second], False, k == DC - 1)
                    ins.then_inc(slots_used, 1)

            def output(b, x):
                trim, Q = trimmed(b), 1 if b % 3 == 1 else 2
                per = len(x) // Q

                def chunk(m, grp, taking, giving):
                    u = U[b, "out"] + m
                    if taking and (m == 0 and b % 3 == 1 or not giving):
                        unit_free(u)
                    for k in range(len(x)):
                        n, t = out_slot(b, m) + 1 - Q + k // per, k % per
                        if taking and t == 0:
                            slot_in(n)
                        if taking and m == 0 and b % 3 != 1 and t == 0:
                            pe.wait_ge(hidl_ready, (b // 3 * 2 + b % 3 // 2) * FC + k + per)
                        if m < DC - split[b] - 1 and k == len(x) - 1:
                            unit_free(u + 1)
                        if m == 0 and b % 3 == 1 and k >= WC:
                            tr = U[b, "tr"] + k - WC
                            pe.wait_ge(psum_free[pair_of(tr)], read_out(tr))
                        ins = tile(u, n, t, x[k][0], x[k][1], grp, k == 0, k == len(x) - 1)
                        if giving and t == per - 1:
                            ins.then_inc(slots_used, 1)
                        elif not giving and k == len(x) - 1:
                            ins.then_inc(half_mm, 1)
                        if m == DC - split[b] and not taking and k == (FH - 1 if b % 3 != 1 else 2):
                            stat_out(b, 0)

                for m in range(DC - split[b]):
                    chunk(m, groups(trim), True, True)
                for s in range(2):
                    for m in range(DC - split[b], DC):
                        chunk(m, groups(trim)[s:s + 1], s == 0, s == 1)

            def partition_sum(u, trim, srcs, s):
                unit_free(u)
                for i, src in enumerate(srcs):
                    for t0, nt, c0 in groups(trim):
                        ins = mm(pair(pair_of(u))[:, c0:c0 + nt], ones, src[:, t0:t0 + nt],
                                 i == 0, i == len(srcs) - 1)
                ins.then_inc(s, 1)

            def half_sum(u, trim, s, srcs, done):
                for i, src in enumerate(srcs):
                    ins = mm(bank(u, trim, s), ones, half(src, trim, s), i == 0, i == len(srcs) - 1)
                ins.then_inc(done, 1)

            def stat_in(b, s):
                if b == s == 0:
                    pe.wait_ge(consts_in, 16)
                pe.wait_ge(hsum_ready, hsum_n(b, s, DC - 1))
                if s == 0:
                    unit_free(U[b, "pre"])
                half_sum(U[b, "pre"], b > 0 and trimmed(b - 1), s, [tmp[4]], stat_pre)

            def stat_out(b, s):
                pe.wait_ge(sum_ready, sum_n(b, DC - 2, s))
                pe.wait_ge(sq_ready, sq_n(b, DC - 1, s))
                if s == 0:
                    unit_free(U[b + 1, "post"])
                half_sum(U[b + 1, "post"], trimmed(b), s, [tmp[4], tmp[(DC - 1) % 2]], stat_post)

            def ffn(b):
                s0 = slot0[b]
                u0, tin = U[b, "gu"], b > 0 and trimmed(b - 1)
                opening(b, u0, s0, tin)
                product(u0 + 3, s0 + 3, tin, leads=True)
                with pe.Fori(0, FC // 2 - 1) as j:
                    for m in range(4):
                        product(u0 + 4 + m, s0 + 4 + m, tin, adv=j * RING, it=j, led=True, leads=True)
                output(b, [(hidh[:, k, :], hidl[:, k, :]) for k in range(FC)])

            def mixer(b):
                l, s0 = b // 3, slot0[b]
                grp = groups(False)
                opening(b, U[b, "xr"], s0, False)
                for c in range(3, WC):
                    product(U[b, "xr"] + c, s0 + S_XR + c, False, led=c > 3, leads=True)
                for c in range(QC):
                    product(U[b, "cq"] + c, s0 + S_CQ + c, False, led=True, leads=c < QC - 1)
                n = s0 + S_GATE
                slot_in(n)
                if l == 0:
                    pe.wait_ge(sp_ready, 1)
                for g in range(2 * WC):
                    u, c = U[b, "gate"] + g, g % WC
                    if g < WC:
                        pe.wait_ge(xcl_ready, WC * l + c + 1)
                    unit_free(u)
                    ins = tile(u, n, g, xch[:, c, :], xcl[:, c, :], grp, True, True)
                    ins.then_inc(gate_mm if g < 2 * WC - 1 else slots_used, 1)
                for c in range(KVC):
                    product(U[b, "ckv"] + c, s0 + S_CKV + c, False)
                pe.wait_ge(qsum_ready, l + 1)
                partition_sum(U[b, "statq"], False, [tmp[0]], stat_mix)
                product(U[b, "kr"], s0 + S_KR, False)
                pe.wait_ge(kvsum_ready, l + 1)
                partition_sum(U[b, "statkv"], False, [tmp[1]], stat_mix)
                for c in range(WC):
                    product(U[b, "gr"] + c, s0 + S_GR + c, False, led=c > 0, leads=c < WC - 1)
                u = U[b, "sel"]
                unit_free(u)
                ukr = U[b, "kr"]
                pe.wait_ge(psum_free[pair_of(ukr)], read_out(ukr))
                for t0, nt, c0 in grp:
                    ins = mm(pair(pair_of(u))[:, c0:c0 + nt], sel[0:2 * ROPE], tmp[4][0:2 * ROPE, t0:t0 + nt],
                             True, True)
                ins.then_inc(sel_mm, 1)
                n = s0 + S_V
                slot_in(n)
                pe.wait_ge(ckvl_ready, KVC * (l + 1))
                r = n % RING
                for i in range(3):
                    u = U[b, "v"] + i
                    unit_free(u)
                    for q in range(2 if i < 2 else 1):
                        t0 = block_of(2 * i + q)[0]
                        o = pair(pair_of(u))[:, q * 512:(q + 1) * 512]
                        for c in range(KVC):
                            wv = slice(c * W, (c + 1) * W)
                            mm(o, ckvh[:, c, t0:t0 + P], whi[:, r, wv], c == 0, False)
                            mm(o, ckvh[:, c, t0:t0 + P], wlo[:, r, wv], False, False)
                            ins = mm(o, ckvl[:, c, t0:t0 + P], whi[:, r, wv], False, c == KVC - 1)
                    ins.then_inc(v_mm if i < 2 else slots_used, 1)
                n = s0 + S_K
                slot_in(n)
                for i in range(HEADS // 2):
                    u = U[b, "k"] + i
                    unit_free(u)
                    for c in range(KVC):
                        ins = tile(u, n, KVC * i + c, ckvh[:, c, :], ckvl[:, c, :], grp, c == 0, c == KVC - 1)
                    ins.then_inc(k_mm if i < HEADS // 2 - 1 else slots_used, 1)
                pe.wait_ge(cql_ready, QC * (l + 1))
                for hd in range(HEADS):
                    u, n = unit_q(b, hd), s0 + S_Q + hd // 2
                    if hd % 2 == 0:
                        slot_in(n)
                    unit_free(u)
                    for c in range(QC):
                        ins = tile(u, n, QC * (hd % 2) + c, cqh[:, c, :], cql[:, c, :], grp,
                                   c == 0, c == QC - 1)
                    ins.then_inc(slots_used if hd % 2 else q_mm, 1)
                    if hd == HEADS // 2 - 1:
                        pe.wait_ge(lsum_ready, 3 * (l + 1))
                        us = U[b, "statl"]
                        partition_sum(us, False, [ig[:, 0, :]], stat_mix)
                attention(b)
                ot = U[b, "tr"]
                n_on = WC * l + n_meta_layers(l) + (0 if trimmed(b) else 1)
                for c in range(WC):
                    u = ot + c
                    unit_free(u)
                    pe.wait_ge(on_ready, n_on + c + 1)
                    pr = pair(pair_of(u))
                    if not trimmed(b):
                        nc.tensor.transpose(pr[:, 512:512 + N_META], osb0[0:N_META, c * P:(c + 1) * P],
                                            ident[0:N_META, 0:N_META])
                    for i in range(NQ):
                        ins = nc.tensor.transpose(pr[:, i * P:(i + 1) * P], osb[:, i, c * P:(c + 1) * P], ident)
                    ins.then_inc(tr_mm, 1)
                pe.wait_ge(yll_ready, WC * (l + 1))
                x = [(ylh[:, k, :], yll[:, k, :]) for k in range(WC)] + \
                    [(xh[:, k, :], xl[:, k, :]) for k in range(WC, DC)]
                output(b, x)

            def attention(b):
                l = b // 3
                last = U[b, "tr"] - 1
                for u in range(last - 3, last + 1):
                    pe.wait_ge(psum_free[pair_of(u)], read_out(u))
                pe.wait_ge(krope_ready, 2 * (l + 1))
                m0, nm = n_meta_layers(l), N_META

                def meta_scores():
                    for hd in range(HEADS):
                        o = meta_turned(hd * nm, nm)
                        mm(o, qt(hd)[:, 0:nm], kt(hd)[:, 0:nm], True, False)
                        ins = mm(o, identb[0:nm, 0:nm], maskb[0:nm, 0:nm], False, True)
                    ins.then_inc(s0_mm, 1)

                def meta_transposes():
                    pe.wait_ge(s0_exp, m0 + 1)
                    for hd in range(HEADS):
                        ins = mm(meta_turned(hd * nm, nm), prob[3][0:nm, hd * nm:(hd + 1) * nm],
                                 ident[0:nm, 0:nm], True, True)
                    ins.then_inc(t0_mm, 1)

                def meta_outputs():
                    pe.wait_ge(t0_copied, 2 * m0 + 1)
                    for hd in range(HEADS):
                        ins = mm(ps[0:nm, 7 * 512 + hd * VD:7 * 512 + (hd + 1) * VD],
                                 probT[2][0:nm, hd * nm:(hd + 1) * nm],
                                 vt[0:nm, 0, hd * VD:(hd + 1) * VD], True, True)
                    ins.then_inc(o0_mm, 1)

                def scores(e):
                    E, hd, i = ITEMS * l + e, e // NQ, e % NQ + 1
                    t0, nk, c = block_of(i)[0], keys_of(i), place(e)
                    if before(e) is not None:
                        copied(before(e))
                    elif e == NQ and not trimmed(b):
                        pe.wait_ge(t0_copied, 2 * m0 + 1)
                    parts = [(0, nk, c)] if i < NQ else [(0, HALF, c), (HALF, HALF, c + 512)]
                    for k0, n, c0 in parts:
                        tail = k0 + n == nk
                        mm(ps[:, c0:c0 + n], qt(hd)[:, t0:t0 + P], kt(hd)[:, k0:k0 + n], True, not tail)
                        if tail:
                            ins = mm(ps[:, c0 + n - P:c0 + n], identb[:, :], maskb[:, :], False, True)
                    ins.then_inc(s_mm, 1)

                def copied(e):
                    full, i = ITEMS // 2 * l + e // NQ * 2, e % NQ + 1
                    if copied_by_act(i):
                        pe.wait_ge(t_act, full + i)
                    else:
                        pe.wait_ge(t_dve, full + i - 2)

                def transposes(e):
                    E, i = ITEMS * l + e, e % NQ + 1
                    pe.wait_ge(prob_ready, E + 1)
                    for j in range(i + 1):
                        k0, c0 = block_of(j)[0], place(e) + j * P
                        ins = nc.tensor.transpose(ps[:, c0:c0 + P], prob[e % 4][:, k0:k0 + P], ident)
                    ins.then_inc(t_mm, 1)

                def outputs(e):
                    hd, i = e // NQ, e % NQ + 1
                    copied(e)
                    if i == 1 and hd >= 2:
                        pe.wait_ge(o_copied, HEADS * l + hd - 1)
                    if e == NQ and not trimmed(b):
                        pe.wait_ge(t0_copied, 2 * m0 + 2)
                    c0 = (hd % 2) * 512 + (i - 1) * VD
                    for j in range(i + 1):
                        kn = block_of(j)[1]
                        ins = mm(pair(3)[:, c0:c0 + VD], probT[e % 3][0:kn, j * P:(j + 1) * P],
                                 vt[0:kn, j, hd * VD:(hd + 1) * VD], j == 0, j == i)
                    ins.then_inc(pv_mm, 1)

                if not trimmed(b):
                    meta_scores()
                for e in range(ITEMS + 3):
                    if e == 2 and not trimmed(b):
                        meta_transposes()
                    if 2 <= e < ITEMS + 2:
                        transposes(e - 2)
                    if e < ITEMS:
                        scores(e)
                    if e == 3 and not trimmed(b):
                        meta_outputs()
                    if e >= 3:
                        outputs(e - 3)
                pe.wait_ge(o_copied, HEADS * (l + 1))

            for b in range(NB):
                if b % 3 == 1:
                    mixer(b)
                else:
                    ffn(b)
            stat_out(NB - 1, 1)


def _feature_columns(v):
    v = v.reshape(v.shape[0], -1, P)
    return v.transpose(0, 2, 1)


def _tiles(w, rows, cols):
    return w.reshape(w.shape[0], rows, P, cols, P).transpose(0, 3, 2, 1, 4).reshape(w.shape[0], cols, P, rows * P)


def _block_diagonal(w):
    L, H, n, _ = w.shape
    o = np.zeros((L, P, H // 2, P), w.dtype)
    for h in range(H):
        s = (h % 2) * n
        o[:, s:s + n, h // 2, s:s + n] = w[:, h]
    return o


def _swap(w):
    n = ROPE // 2
    return np.concatenate([w[..., n:], w[..., :n]], axis=-1)


def _consts():
    c = np.zeros((P, NCONST), np.float32)
    c[:, C_ID:C_ID + P] = np.eye(P)
    c[:, C_ONE:C_ONE + P] = 1.0
    for i in range(ROPE):
        for q in range(P // ROPE):
            c[i, C_SEL + q * ROPE + i] = 1.0
            c[ROPE + i, C_SEL + q * ROPE + i] = 1.0
    c[:, C_MASK:C_MASK + P] = np.triu(np.full((P, P), MASKED), 1)
    c[:, C_EPS] = EPS
    c[:, C_LNS] = -0.5 * np.log(NOPE + ROPE)
    return c


def _rope():
    inv = (1.0 / (np.float32(ROPE_THETA) ** (np.arange(0, ROPE, 2, dtype=np.float32) / np.float32(ROPE))))
    ang = np.arange(T, dtype=np.float32)[None, :] * inv.astype(np.float32)[:, None]
    cos, sin = np.cos(ang), np.sin(ang)
    factors = np.concatenate([cos, cos, -sin, sin], axis=0)
    one = np.ones((NOPE, T))
    return np.stack([np.concatenate([one, factors]), np.concatenate([factors, one])]).astype(np.float32)


def kernel(**inputs):
    import concourse.bacc as bacc
    from concourse.bass_utils import run_bass_kernel_spmd

    g = {k: np.asarray(v) for k, v in inputs.items()}
    depth, d_ff = g["ffn1_w_gate"].shape[0], g["ffn1_w_gate"].shape[2]
    FC = d_ff // P
    arrays = {"consts": _consts(), "rope": _rope()}
    x = np.concatenate([g["meta_tokens"], g["x"][0]], axis=0)
    arrays["x"] = x.T.reshape(DC, P, T)
    arrays["params"] = np.concatenate([_feature_columns(g[n]) for n, _ in PARAMS], axis=2).transpose(1, 0, 2)
    for f in ("ffn1", "ffn2"):
        arrays[f + "_gate"] = _tiles(g[f + "_w_gate"], DC, FC)
        arrays[f + "_up"] = _tiles(g[f + "_w_up"], DC, FC)
        arrays[f + "_down"] = _tiles(g[f + "_w_down"], FC, DC).reshape(depth, DC, P, 2, FC // 2 * P)\
            .transpose(0, 1, 3, 2, 4)
    w = g["w_in"]
    kr = w[:, :, 2 * W + QL + KVL:]
    w = np.concatenate([w[:, :, 0:W], w[:, :, 2 * W:2 * W + QL + KVL], kr, _swap(kr), kr, _swap(kr),
                        w[:, :, W:2 * W]], axis=2)
    arrays["w_in"] = _tiles(w, DC, w.shape[2] // P)
    arrays["w_gates"] = np.concatenate([_block_diagonal(g["lru_w_a"]), _block_diagonal(g["lru_w_x"])],
                                       axis=2).reshape(depth, P, 2 * WC * P)
    q = g["mla_w_uq"].reshape(depth, QL, HEADS, NOPE + ROPE)
    nope, rope = q[..., :NOPE], q[..., NOPE:]
    even = np.concatenate([nope, rope, _swap(rope)], axis=-1)
    odd = np.concatenate([rope, _swap(rope), nope], axis=-1)
    q = np.stack([even[:, :, 0::2], odd[:, :, 1::2]], axis=3).reshape(depth, QL, HEADS * P)
    arrays["w_q"] = _tiles(q, QC, HEADS).reshape(depth, HEADS // 2, 2, P, QC * P)\
        .transpose(0, 1, 3, 2, 4).reshape(depth, HEADS // 2, P, 2 * QC * P)
    kv = g["mla_w_ukv"].reshape(depth, KVL, HEADS, NOPE + VD)
    k = kv[..., :NOPE].reshape(depth, KVL, HEADS * NOPE)
    v = kv[..., NOPE:].reshape(depth, KVL, HEADS * VD)
    arrays["w_k"] = _tiles(k, KVC, HEADS // 2).transpose(0, 2, 1, 3).reshape(depth, P, -1)
    arrays["w_v"] = v.reshape(depth, KVC, P, W).transpose(0, 2, 1, 3).reshape(depth, P, -1)
    arrays["w_out"] = _tiles(g["w_out"], DC, DC)

    nc = bacc.Bacc("TRN2", target_bir_lowering=False, num_devices=1, dynamic_dma_scratch_size=64)
    arrays = {f"in_{n}": np.ascontiguousarray(v) for n, v in arrays.items()}
    a = {n[3:]: nc.dram_tensor(n, v.shape, mybir.dt.from_np(v.dtype), kind="ExternalInput").ap()
         for n, v in arrays.items()}
    out = nc.dram_tensor("out_t", (DC, P, SEQ), F32, kind="ExternalOutput").ap()
    build_program(nc, a, out, depth, d_ff)
    r = run_bass_kernel_spmd(nc, [arrays], core_ids=[0])
    o = r.results[0]["out_t"]
    return np.ascontiguousarray(o.reshape(D, SEQ).T)[None]
```
